# Optimizing a Trainium2 kernel written in Bass

```python
import math
import jax, jax.numpy as jnp
from jax import lax
import numpy as np

D_MODEL = 1024
BATCH = 1
SEQ = 512
DEPTH = 1

HEAD_DIM = 64
DIFF_HEADS = 4
DIFF_VDIM = 2 * HEAD_DIM
DIFF_WIDTH = DIFF_HEADS * DIFF_VDIM
DIL_HEADS = 4
DIL_WIDTH = DIL_HEADS * HEAD_DIM
DIL_WINDOWS = (128, 512, 2048)
DIL_DILATIONS = (1, 4, 16)
DIL_NKEYS = DIL_WINDOWS[0] // DIL_DILATIONS[0] + 1
MEM_HEADS = 4
MEM_WIDTH = MEM_HEADS * HEAD_DIM
N_MEM = 256
D_MIX = DIFF_WIDTH + DIL_WIDTH + MEM_WIDTH
C_DIFF_Q = 0
C_DIFF_K = C_DIFF_Q + DIFF_WIDTH
C_DIFF_V = C_DIFF_K + DIFF_WIDTH
C_DIL_Q = C_DIFF_V + DIFF_WIDTH
C_DIL_K = C_DIL_Q + DIL_WIDTH
C_DIL_V = C_DIL_K + DIL_WIDTH
C_MEM_Q = C_DIL_V + DIL_WIDTH
D_IN = C_MEM_Q + MEM_WIDTH
Q_BLOCK = 128
DIL_Q_BLOCK = 64
N_EXPERTS = 32
TOP_K = 4
D_FF = D_MODEL
SWIGLU_ALPHA = 1.702
SWIGLU_LIMIT = 7.0
MOE_BLOCK = 256
NORM_EPS = 1e-5

kernel_name = "hymba_diff_dilated_mem_moe_block"

def rms_norm(x, g):
    xf = x.astype(jnp.float32)
    y = xf * lax.rsqrt(jnp.mean(xf * xf, axis=-1, keepdims=True) + NORM_EPS)
    return (y * g.astype(jnp.float32)).astype(x.dtype)

def alibi_slopes():
    n = DIFF_HEADS + DIL_HEADS
    s = 2.0 ** (-8.0 * (jnp.arange(n, dtype=jnp.float32) + 1.0) / n)
    return s[0::2], s[1::2]

def dilated_distances():
    r = jnp.array(DIL_DILATIONS, dtype=jnp.int32)
    return jnp.arange(DIL_NKEYS, dtype=jnp.int32)[None, :] * r[:, None]

def split_heads(t, n_heads, d):
    b, s, _ = t.shape
    return t.reshape(b, s, n_heads, d).transpose(0, 2, 1, 3)

def merge_heads(t):
    b, h, s, d = t.shape
    return t.transpose(0, 2, 1, 3).reshape(b, s, h * d)

def diff_attention(q1, q2, k1, k2, v, slopes, lam):
    b, h, s, dh = q1.shape
    scale = dh ** -0.5
    kpos = jnp.arange(s)

    def block(i):
        start = i * Q_BLOCK
        qb1 = lax.dynamic_slice_in_dim(q1, start, Q_BLOCK, axis=2)
        qb2 = lax.dynamic_slice_in_dim(q2, start, Q_BLOCK, axis=2)
        qpos = start + jnp.arange(Q_BLOCK)
        dist = qpos[:, None] - kpos[None, :]
        causal = dist >= 0
        bias = -slopes[:, None, None] * dist.astype(jnp.float32)

        def probs(qb, k):
            sc = jnp.einsum('bhqd,bhkd->bhqk', qb, k).astype(jnp.float32) * scale + bias
            return jax.nn.softmax(jnp.where(causal, sc, -jnp.inf), axis=-1)

        a = probs(qb1, k1) - lam * probs(qb2, k2)
        return jnp.einsum('bhqk,bhkd->bhqd', a.astype(v.dtype), v)

    o = lax.map(block, jnp.arange(s // Q_BLOCK))
    return o.transpose(1, 2, 0, 3, 4).reshape(b, h, s, v.shape[-1])

def dilated_attention(q, k, v, slopes):
    b, h, s, dh = q.shape
    scale = dh ** -0.5
    dist = dilated_distances()
    bias = -slopes[:, None, None, None] * dist.astype(jnp.float32)

    def block(i):
        start = i * DIL_Q_BLOCK
        qb = lax.dynamic_slice_in_dim(q, start, DIL_Q_BLOCK, axis=2)
        qpos = start + jnp.arange(DIL_Q_BLOCK)
        kidx = qpos[:, None, None] - dist[None]
        valid = kidx >= 0
        kidx = jnp.maximum(kidx, 0)
        kg = jnp.take(k, kidx, axis=2, mode='clip')
        vg = jnp.take(v, kidx, axis=2, mode='clip')
        sc = jnp.einsum('bhqd,bhqnkd->bhqnk', qb, kg).astype(jnp.float32) * scale + bias
        sc = jnp.where(valid, sc, -jnp.inf)
        m = jnp.max(sc, axis=-1, keepdims=True)
        p = jnp.exp(sc - m)
        denom = jnp.sum(p, axis=-1)
        o = jnp.einsum('bhqnk,bhqnkd->bhqnd', p.astype(v.dtype), vg).astype(jnp.float32) / denom[..., None]
        w = jax.nn.softmax(m[..., 0] + jnp.log(denom), axis=-1)
        return jnp.einsum('bhqn,bhqnd->bhqd', w, o)

    o = lax.map(block, jnp.arange(s // DIL_Q_BLOCK))
    return o.transpose(1, 2, 0, 3, 4).reshape(b, h, s, dh)

def memory_attention(q, mk, mv):
    scale = q.shape[-1] ** -0.5
    sc = jnp.einsum('bhsd,bhmd->bhsm', q, mk).astype(jnp.float32) * scale
    a = jax.nn.softmax(sc, axis=-1)
    return jnp.einsum('bhsm,bhmd->bhsd', a.astype(mv.dtype), mv)

def moe_ffn(h, w_router, b_router, w_gu, b_gu, w_dn, b_dn):
    b, s, d = h.shape
    t = b * s
    xf = h.reshape(t, d)
    logits = (xf @ w_router + b_router).astype(jnp.float32)
    top_v, top_e = lax.top_k(logits, TOP_K)
    gates = jax.nn.softmax(top_v, axis=-1)
    n_assign = t * TOP_K
    e_flat = top_e.reshape(-1)
    g_flat = gates.reshape(-1)
    tok_flat = jnp.arange(n_assign, dtype=jnp.int32) // TOP_K
    order = jnp.argsort(e_flat, stable=True)
    e_sorted = e_flat[order]
    counts = jnp.bincount(e_flat, length=N_EXPERTS)
    padded = (counts + MOE_BLOCK - 1) // MOE_BLOCK * MOE_BLOCK
    pad_end = jnp.cumsum(padded)
    pad_start = pad_end - padded
    start = jnp.cumsum(counts) - counts
    rank = jnp.arange(n_assign, dtype=jnp.int32) - start[e_sorted]
    dest = pad_start[e_sorted] + rank
    n_blocks = -(-n_assign // MOE_BLOCK) + N_EXPERTS
    n_rows = n_blocks * MOE_BLOCK
    row_tok = jnp.zeros((n_rows,), jnp.int32).at[dest].set(tok_flat[order])
    row_gate = jnp.zeros((n_rows,), jnp.float32).at[dest].set(g_flat[order])
    block_expert = jnp.minimum(
        jnp.searchsorted(pad_end, jnp.arange(n_blocks) * MOE_BLOCK, side='right'), N_EXPERTS - 1)
    xb = xf[row_tok].reshape(n_blocks, MOE_BLOCK, d)

    def expert_block(args):
        xe, e = args
        gu = xe @ w_gu[e] + b_gu[e]
        gate = jnp.minimum(gu[..., 0::2], SWIGLU_LIMIT)
        up = jnp.clip(gu[..., 1::2], -SWIGLU_LIMIT, SWIGLU_LIMIT)
        act = (up + 1.0) * (gate * jax.nn.sigmoid(gate * SWIGLU_ALPHA))
        return act @ w_dn[e] + b_dn[e]

    yb = lax.map(expert_block, (xb, block_expert))
    out = jnp.zeros((t, d), jnp.float32).at[row_tok].add(
        yb.reshape(n_rows, d).astype(jnp.float32) * row_gate[:, None])
    return out.reshape(b, s, d).astype(h.dtype)

def setup_inputs(seed: int = 0) -> dict:
    key = jax.random.key(seed)
    ks = jax.random.split(key, 18)
    f32 = jnp.float32

    def nrm(k, shape, scale):
        return jax.random.normal(k, shape, f32) * scale

    return {
        "x": nrm(ks[0], (BATCH, SEQ, D_MODEL), 1.0),
        "mem": nrm(ks[1], (BATCH, N_MEM, D_MODEL), 1.0),
        "attn_norm_g": 1.0 + nrm(ks[2], (DEPTH, D_MODEL), 0.02),
        "mem_norm_g": 1.0 + nrm(ks[3], (DEPTH, D_MODEL), 0.02),
        "w_in": nrm(ks[4], (DEPTH, D_MODEL, D_IN), D_MODEL ** -0.5),
        "diff_lambda_qk": nrm(ks[5], (DEPTH, 4, HEAD_DIM), 0.1),
        "diff_subln_g": 1.0 + nrm(ks[6], (DEPTH, DIFF_VDIM), 0.02),
        "w_mem_kv": nrm(ks[7], (DEPTH, D_MODEL, 2 * MEM_WIDTH), D_MODEL ** -0.5),
        "w_out": nrm(ks[8], (DEPTH, D_MIX, D_MODEL), D_MIX ** -0.5),
        "ffn_norm_g": 1.0 + nrm(ks[9], (DEPTH, D_MODEL), 0.02),
        "w_router": nrm(ks[10], (DEPTH, D_MODEL, N_EXPERTS), D_MODEL ** -0.5),
        "b_router": nrm(ks[11], (DEPTH, N_EXPERTS), 0.01),
        "w_gate_up": nrm(ks[12], (DEPTH, N_EXPERTS, D_MODEL, 2 * D_FF), D_MODEL ** -0.5),
        "b_gate_up": nrm(ks[13], (DEPTH, N_EXPERTS, 2 * D_FF), 0.01),
        "w_down": nrm(ks[14], (DEPTH, N_EXPERTS, D_FF, D_MODEL), D_FF ** -0.5),
        "b_down": nrm(ks[15], (DEPTH, N_EXPERTS, D_MODEL), 0.01),
        "final_norm_g": 1.0 + nrm(ks[16], (D_MODEL,), 0.02),
    }

def reference(x, mem, attn_norm_g, mem_norm_g, w_in, diff_lambda_qk, diff_subln_g, w_mem_kv,
              w_out, ffn_norm_g, w_router, b_router, w_gate_up, b_gate_up, w_down, b_down,
              final_norm_g):
    b, s, _ = x.shape
    diff_slopes, dil_slopes = alibi_slopes()
    for l in range(DEPTH):
        h = rms_norm(x, attn_norm_g[l])
        p = h @ w_in[l]

        lam_init = 0.8 - 0.6 * math.exp(-0.3 * l)
        lv = diff_lambda_qk[l].astype(jnp.float32)
        lam = jnp.exp(jnp.sum(lv[0] * lv[1])) - jnp.exp(jnp.sum(lv[2] * lv[3])) + lam_init
        dq = p[..., C_DIFF_Q:C_DIFF_K].reshape(b, s, DIFF_HEADS, 2, HEAD_DIM).transpose(0, 2, 3, 1, 4)
        dk = p[..., C_DIFF_K:C_DIFF_V].reshape(b, s, DIFF_HEADS, 2, HEAD_DIM).transpose(0, 2, 3, 1, 4)
        dv = split_heads(p[..., C_DIFF_V:C_DIL_Q], DIFF_HEADS, DIFF_VDIM)
        o_diff = diff_attention(dq[:, :, 0], dq[:, :, 1], dk[:, :, 0], dk[:, :, 1], dv, diff_slopes, lam)
        o_diff = rms_norm(o_diff, diff_subln_g[l]) * (1.0 - lam_init)
        o_diff = merge_heads(o_diff.astype(x.dtype))

        lq = split_heads(p[..., C_DIL_Q:C_DIL_K], DIL_HEADS, HEAD_DIM)
        lk = split_heads(p[..., C_DIL_K:C_DIL_V], DIL_HEADS, HEAD_DIM)
        lvv = split_heads(p[..., C_DIL_V:C_MEM_Q], DIL_HEADS, HEAD_DIM)
        o_dil = merge_heads(dilated_attention(lq, lk, lvv, dil_slopes).astype(x.dtype))

        mq = split_heads(p[..., C_MEM_Q:D_IN], MEM_HEADS, HEAD_DIM)
        mkv = rms_norm(mem, mem_norm_g[l]) @ w_mem_kv[l]
        mk = split_heads(mkv[..., :MEM_WIDTH], MEM_HEADS, HEAD_DIM)
        mv = split_heads(mkv[..., MEM_WIDTH:], MEM_HEADS, HEAD_DIM)
        o_mem = merge_heads(memory_attention(mq, mk, mv).astype(x.dtype))

        mix = jnp.concatenate([o_diff, o_dil, o_mem], axis=-1)
        x = x + mix @ w_out[l]

        x = x + moe_ffn(rms_norm(x, ffn_norm_g[l]), w_router[l], b_router[l],
                        w_gate_up[l], b_gate_up[l], w_down[l], b_down[l])
    return rms_norm(x, final_norm_g)


_drawn_inputs = setup_inputs


def setup_inputs(seed=0):
    import zlib

    import numpy as np

    out = dict(_drawn_inputs(seed))
    spreads = {}
    factors = {'mem_norm_g': 6.366,
     'b_gate_up': 23.871,
     'b_down': 27.567,
     'final_norm_g': 8.171,
     'diff_lambda_qk': 3.029,
     'diff_subln_g': 6.07,
     'ffn_norm_g': 3.053,
     'b_router': 4.22}
    for name, (base, spread) in spreads.items():
        noise = np.random.default_rng([zlib.crc32(name.encode()), seed]).standard_normal(out[name].shape)
        drawn = base * np.exp(spread * noise) if base else spread * noise
        out[name] = __import__('jax').numpy.asarray(drawn.astype(out[name].dtype))
    for name, factor in factors.items():
        out[name] = (out[name] * factor).astype(out[name].dtype)
    return out
```

```python
import math
from contextlib import ExitStack

import numpy as np

import concourse.bass as bass
from concourse import mybir

F32 = mybir.dt.float32
F32R = mybir.dt.float32r
I32 = mybir.dt.int32
U32 = mybir.dt.uint32
ALU = mybir.AluOpType
ACT = mybir.ActivationFunctionType
AX_X = mybir.AxisListType.X

P = 128
D = 1024
KT = D // P
S = 512
NT = S // P
MEM = 256
DH = 64
HEADS = 4
DIL = ((128, 1), (512, 4), (2048, 16))
E = 32
TOPK = 4
FF = 1024
LIMIT = 7.0
ALPHA = 1.702
EPS = 1e-5
LAM_INIT = 0.8 - 0.6 * math.exp(-0.3 * 0)
SCALE = DH ** -0.5
NEG = -1e30

UC = 512
HALF = KT // 2 * UC
PHASE_A_UNITS = 8
MAX_BLOCKS = 48
MAX_LOOPS = 46
ROWS = S + P

C_IDENT, C_TRI, C_ONES, C_IOTA = 0, P, 2 * P, 3 * P
C_TOK = 4 * P
C_IDLE = C_TOK + NT
C_ROWMOD = C_IDLE + 1
N_CONST = C_ROWMOD + 1


def position_tables():
    p = np.arange(P)[:, None]
    dist = p - (np.arange(S)[None, :] - (S - P))
    slopes = [2.0 ** (-8.0 * (i + 1) / 8) for i in range(8)]
    out = np.full((8, P, S), NEG, np.float32)
    for h in range(HEADS):
        out[h] = np.where(dist >= 0, -slopes[2 * h] * dist / SCALE, NEG)
        count = sum(((dist % r == 0) & (dist <= w)).astype(int) for w, r in DIL) * (dist >= 0)
        term = (-slopes[2 * h + 1] * dist + np.log(np.maximum(count, 1))) / SCALE
        out[HEADS + h] = np.where(count > 0, term, NEG)
    return out.astype(np.float32)


def constants():
    c = np.zeros((P, N_CONST), np.float32)
    p = np.arange(P)
    c[:, C_IDENT:C_IDENT + P] = np.eye(P)
    c[:, C_TRI:C_TRI + P] = p[:, None] < p[None, :]
    c[:, C_ONES:C_ONES + P] = 1.0
    c[:, C_IOTA:C_IOTA + P] = p[None, :]
    for t in range(NT):
        c[:, C_TOK + t] = t * P + p + 1
    c[:, C_IDLE] = S + p + 1
    c[:, C_ROWMOD] = np.where(p < 2 * E, p % E, -1)
    return c


def attention_tasks():
    tasks, late = [], []
    for qb in range(NT):
        heads = [(kind, h, qb) for kind in ("diff", "dil", "mem") for h in range(HEADS)]
        tasks += heads[:1] + late + heads[1:]
        late = [("mix", 0, qb), ("mix", 1, qb)]
    return tasks + [None] + late


def hymba_layer(nc, x, mem, attn_norm_g, mem_norm_g, w_in, diff_lambda_qk, diff_subln_g, w_mem_kv,
                w_out, ffn_norm_g, w_router, b_router, w_gate_up, b_gate_up, w_down, b_down,
                final_norm_g, const, postab, out):
    x_rows = x.rearrange("b (t p) d -> p (b t) d", p=P)
    mem_rows = mem.rearrange("b (t p) d -> p (b t) d", p=P)
    out_rows = out.rearrange("b (t p) d -> p (b t) d", p=P)
    h_dram = nc.dram_tensor("normed_rows", (S, D), F32).ap()
    sum_dram = nc.dram_tensor("sum_rows", (ROWS, D), F32).ap()

    def weight_columns(w, c):
        return w.rearrange("(k p) n -> p k n", p=P)[:, :, c * UC:(c + 1) * UC]

    phase_a = [weight_columns(w_mem_kv[0], 0)] + [weight_columns(w_in[0], c) for c in range(5)] \
        + [weight_columns(w_out[0], c) for c in range(2)]
    gu_dram = w_gate_up[0].rearrange("e (k p) n -> e p k n", p=P)
    dn_dram = w_down[0].rearrange("e (k p) n -> e p k n", p=P)

    with ExitStack() as ctx:
        def sb(name, shape, dt):
            return ctx.enter_context(nc.sbuf_tensor(name, shape, dt))

        def sem(name):
            return ctx.enter_context(nc.semaphore(name))

        raw = sb("raw", [P, 3, KT * UC], F32)
        w_hi = sb("w_hi", [P, 4, HALF], F32R)
        w_lo = sb("w_lo", [P, 4, HALF], F32R)
        R = sb("turned", [P, 2 * KT * S], F32R)
        F = sb("arena", [P, 15360], F32)
        cst = sb("cst", [P, N_CONST], F32)
        gains = sb("gains", [P, 3 * KT + 1], F32)
        stat = sb("stat", [P, 8, 8], F32)
        nrm = sb("nrm", [P, 4, 4], F32)
        lamw = sb("lamw", [P, 8], F32)
        psum = [ctx.enter_context(nc.psum_tensor(f"bank{i}", [P, 512], F32)) for i in range(8)]

        ident = cst[:, C_IDENT:C_IDENT + P]
        tri = cst[:, C_TRI:C_TRI + P]
        ones = cst[:, C_ONES:C_ONES + P]
        iota = cst[:, C_IOTA:C_IOTA + P]
        g_attn, g_mem, g_ffn = (gains[:, i * KT:(i + 1) * KT] for i in range(3))
        g_mix = gains[:, 3 * KT:3 * KT + 1]

        act_hi = R[:, 0:KT * S].rearrange("p (k s) -> p k s", k=KT)
        act_lo = R[:, KT * S:].rearrange("p (k s) -> p k s", k=KT)

        xr = F[:, 0:4096].rearrange("p (t d) -> p t d", t=NT)
        mr = F[:, 4096:6144].rearrange("p (t d) -> p t d", t=2)
        junk = F[:, 13312:14336]
        lam_in = F[:, 14336:14592].rearrange("p (a d) -> p a d", a=4)
        qk = F[:, 0:7168].rearrange("p (i s) -> p i s", i=14)
        dil_v = F[:, 7168:8192].rearrange("p (t n) -> p t n", t=NT)
        mem_v = F[:, 8192:8704].rearrange("p (t n) -> p t n", t=2)
        mem_k = F[:, 8704:9216].rearrange("p (t n) -> p t n", t=2)
        pos = F[:, 9216:13312].rearrange("p (h u) -> p h u", h=8)
        probs = F[:, 13312:15360].rearrange("p (i j s) -> p i j s", i=2, j=2)
        diff_v = raw[:, 2, 0:2048].rearrange("p (t n) -> p t n", t=NT)
        pt = raw[:, 2, 2048:3072].rearrange("p (i s) -> p i s", i=2)
        mix = raw[:, 2, 3072:4096]

        xn = F[:, 4096:8192].rearrange("p (t d) -> p t d", t=NT)
        hT = F[:, 8192:10240].rearrange("p (i k s) -> p i k s", i=2, k=KT)
        w_rt = F[:, 10240:10496].rearrange("p (k e) -> p k e", k=KT)
        at = [10496]

        def small(n):
            at[0] += n
            assert at[0] <= 12288
            return F[:, at[0] - n:at[0]]

        lg = small(NT * E).rearrange("p (t e) -> p t e", t=NT)
        top = small(NT * 8).rearrange("p (t k) -> p t k", t=NT)
        top_i = small(NT * 8).bitcast(U32).rearrange("p (t k) -> p t k", t=NT)
        top_f = small(NT * 8).rearrange("p (t k) -> p t k", t=NT)
        ntop = small(NT)
        gate_e = small(NT * TOPK).rearrange("p (t k) -> p t k", t=NT)
        gate_s = small(NT)
        picked = small(NT * TOPK * E).rearrange("p (t k e) -> p t k e", t=NT, k=TOPK)
        chosen = small(NT * E).rearrange("p (t e) -> p t e", t=NT)
        n_blk = small(E)
        cum = small(4 * E).rearrange("p (i e) -> p i e", i=2)
        b_start = small(E)
        slots = small(NT * E).rearrange("p (t e) -> p t e", t=NT)
        slot_f = small(NT * TOPK)
        slot_i = small(NT * TOPK).bitcast(I32)
        loc_i = small(NT * TOPK).bitcast(I32)
        blk_i = small(NT * TOPK).bitcast(I32)
        loc_f = small(NT * TOPK)
        blk_f = small(NT * TOPK)
        br_row = small(E)[0:1, :]
        lane_hot = F[:, 12288:14336].rearrange("p (i s) -> p i s", i=NT * TOPK)
        blk_hot = F[:, 8192:9728].rearrange("p (i j b) -> p i j b", i=NT * TOPK, j=2)
        e_cmp = F[:, 8192:9728].rearrange("p (b e) -> p b e", b=MAX_BLOCKS)
        tabs = F[:, 14336:14336 + 8 * MAX_BLOCKS].rearrange("p (i b) -> p i b", i=8)
        tok_f, gate_t, exp_f, idle_f = (tabs[:, i, :] for i in range(4))
        sum_row_i = tabs[:, 4, :].bitcast(I32)
        tok_i = tabs[:, 5, :].bitcast(I32)
        exp_i = tabs[:, 6, :].bitcast(I32)
        loops_i = tabs[:, 7, 0:1].bitcast(I32)
        idx_gather = F[:, 15000:15001].bitcast(I32)
        idx_scatter = F[:, 15001:15002].bitcast(I32)

        bias_in = F[0:2 * E, 0:3 * FF]
        h_row = F[:, 4096:5120]
        act = F[:, 5120:6144]
        y_row = F[:, 6144:7168]
        gate_c, up_c, prod_c, sig_c = (F[:, 7168 + 512 * i:7680 + 512 * i].rearrange("p (i n) -> p i n", i=2)
                                       for i in range(4))
        g_final = F[:, 9728:10752]
        hx, lx = (R[:, i * D:(i + 1) * D].rearrange("p (k s) -> p k s", k=KT) for i in (0, 1))
        ha, la = (R[:, i * D:(i + 1) * D].rearrange("p (k s) -> p k s", k=KT) for i in (2, 3))
        bias = R[:, 4 * D:7 * D]
        pick = R[:, 7 * D:7 * D + P]

        const_in, gains_in, mem_in, x_in, pos_in, lam_in_s = (
            sem(n) for n in ("const_in", "gains_in", "mem_in", "x_in", "pos_in", "lam_in_s"))
        raw_in = [sem(f"raw_in{i}") for i in range(3)]
        hi_ready, lo_ready, half_used = sem("hi_ready"), sem("lo_ready"), sem("half_used")
        dve_seq = sem("dve_seq")
        squares = sem("squares")
        normed = sem("normed")
        turn_in, turn_hi, turn_lo = sem("turn_in"), sem("turn_hi"), sem("turn_lo")
        proj_in, proj_out = sem("proj_in"), sem("proj_out")
        lam_dots, lam_exp, lam_ready = sem("lam_dots"), sem("lam_exp"), sem("lam_ready")
        sc_ready, max_done, exp_done, prob_ready = (
            sem(n) for n in ("sc_ready", "max_done", "exp_done", "prob_ready"))
        pt_in, pt_out, mix_lo, pv_done, out_done = (
            sem(n) for n in ("pt_in", "pt_out", "mix_lo", "pv_done", "out_done"))
        x_again, wo_done, x1_ready = sem("x_again"), sem("wo_done"), sem("x1_ready")
        rows_out = sem("rows_out")
        router_in, router_g = sem("router_in"), sem("router_g")
        ht_in, ht_out, lg_in, lg_out = sem("ht_in"), sem("ht_out"), sem("lg_in"), sem("lg_out")
        top_ready, gates_e = sem("top_ready"), sem("gates_e")
        gather_go, scatter_go = sem("gather_go"), sem("scatter_go")
        chosen_ready, rank_in, hot_ready, tab_in, tab_ready = (
            sem(n) for n in ("chosen_ready", "rank_in", "hot_ready", "tab_in", "tab_ready"))
        bias_in_s, bias_ready = sem("bias_in_s"), sem("bias_ready")
        idx_ready, h_in, y_sent, x1_sent = (sem(n) for n in ("idx_ready", "h_in", "y_sent", "x1_sent"))
        xtp_done, xhi_ready, xlo_ready = sem("xtp_done"), sem("xhi_ready"), sem("xlo_ready")
        atp_done, ahi_ready, alo_ready = sem("atp_done"), sem("ahi_ready"), sem("alo_ready")
        pick_ready, ybias_done = sem("pick_ready"), sem("ybias_done")
        gu_done, gu_free, gate_ready, sig_ready, prod_ready, act_ready = (
            sem(n) for n in ("gu_done", "gu_free", "gate_ready", "sig_ready", "prod_ready", "act_ready"))
        y_free = sem("y_free")
        gf_in, fin_in, fin_out = sem("gf_in"), [sem(f"fin_in{t}") for t in range(NT)], sem("fin_out")
        out_sent = sem("out_sent")

        tasks = attention_tasks()
        real = {t: i for i, t in enumerate(t for t in tasks if t and t[0] != "mix")}
        turned = {t: i for i, t in enumerate(t for t in tasks if t)}
        by_turn = list(turned)
        NR, NTURN = len(real), len(turned)
        LAG_T, LAG_V = 2, 3
        STEPS = len(tasks) + LAG_V

        def task(i):
            return tasks[i] if 0 <= i < len(tasks) else None

        def is_real(t):
            return t is not None and t[0] != "mix"

        def n_keys(t):
            return MEM if t[0] == "mem" else P * (t[2] + 1)

        def turned_index(r):
            return turned[list(real)[r]]

        TILES = [(0, MEM, True, 0, 0), (0, MEM, True, P, 0), (0, MEM, False, MEM, 0), (0, MEM, False, MEM, P)]
        for u in (1, 2, 3, 4):
            TILES += [(u, 512, False, 0, t * P) if u == 3 else (u, S, True, t * P, 0) for t in range(NT)]
        TILES += [(5, 256, False, 0, t * P) for t in range(NT)] + [(5, S, True, 256 + j * P, 0) for j in range(2)]
        N_IN = len(TILES)
        TILES += [(u, 512, False, 0, t * P) for u in (6, 7) for t in range(NT)]
        TILES = [t + (n + 1 == len(TILES) or TILES[n + 1][0] != t[0],) for n, t in enumerate(TILES)]

        def proj_bank(n):
            return n % 4 if n < N_IN else n - N_IN

        def wait_tile(eng, n):
            if TILES[n][5]:
                eng.wait_ge(half_used, 2 * TILES[n][0] + 2)
            else:
                eng.wait_ge(proj_in, sum(not t[5] for t in TILES[:n + 1]))

        def raw_slot(m_static):
            return m_static % 3

        def raw_value(m_static, b6=0):
            s = m_static % 3
            return 16 * ((4 if s < 2 else 0) + m_static // 3 + 1) + 32 * b6

        block = ctx.enter_context(nc.Block())

        @block.sync
        def _(sp):
            sp.dma_start(cst[:, :], const).then_inc(const_in, 16)
            sp.dma_start(mr, mem_rows).then_inc(mem_in, 16)
            sp.dma_start(raw[:, 0, :].rearrange("p (k n) -> p k n", k=KT), phase_a[0]).then_inc(raw_in[0], 16)
            sp.dma_start(xr, x_rows).then_inc(x_in, 16)
            for u in range(1, PHASE_A_UNITS):
                if u >= 2:
                    sp.wait_ge(lo_ready, 2 * (u - 2) + 2)
                sp.dma_start(raw[:, u % 2, :].rearrange("p (k n) -> p k n", k=KT),
                             phase_a[u]).then_inc(raw_in[u % 2], 16)
                if u == 1:
                    sp.dma_start(pos, postab.rearrange("h p u -> p h u")).then_inc(pos_in, 16)
            sp.wait_ge(sc_ready, NR)
            sp.dma_start(xr, x_rows).then_inc(x_again, 16)

            def gate_up(e, c, m):
                sp.dma_start(raw[:, raw_slot(m), :].rearrange("p (k n) -> p k n", k=KT),
                             gu_dram[e, :, :, c * UC:(c + 1) * UC]).then_inc(raw_in[raw_slot(m)], 16)

            def down(e, c, m):
                sp.dma_start(raw[:, raw_slot(m), :].rearrange("p (k n) -> p k n", k=KT // 2),
                             dn_dram[e, :, c * (KT // 2):(c + 1) * (KT // 2), :]).then_inc(raw_in[raw_slot(m)], 16)

            sp.wait_ge(lo_ready, 14)
            gate_up(0, 0, 0)
            sp.wait_ge(lo_ready, 16)
            gate_up(0, 1, 1)
            sp.wait_ge(mix_lo, 2 * NT)
            sp.wait_ge(pv_done, NR)
            gate_up(0, 2, 2)
            sp.wait_ge(wo_done, 2 * NT)
            sp.dma_start(sum_dram[0:S, :].rearrange("(t p) d -> p t d", p=P), xr).then_inc(x1_sent, 16)
            for t in range(NT):
                sp.wait_ge(normed, 6 + t + 1)
                sp.dma_start(h_dram[t * P:(t + 1) * P, :], xn[:, t, :]).then_inc(rows_out, 16)
            sp.wait_ge(lo_ready, 18)
            gate_up(0, 3, 3)
            sp.wait_ge(tab_ready, 1)
            loops = sp.value_load(loops_i[0:1, :], min_val=E - 1, max_val=MAX_LOOPS)

            with sp.Fori(0, loops) as b:
                e = sp.value_load(exp_i[0:1, bass.ds(b, 1)], min_val=0, max_val=E - 1)
                e_next = sp.value_load(exp_i[0:1, bass.ds(b + 1, 1)], min_val=0, max_val=E - 1)
                for j in range(6):
                    sp.wait_ge(lo_ready, b * 12 + (20 + 2 * j))
                    m = 4 + j
                    if j in (1, 2):
                        sp.dma_start(raw[:, raw_slot(m), :].rearrange("p (k n) -> p k n", k=KT // 2),
                                     dn_dram[bass.ds(e, 1), :, (j - 1) * 4:j * 4, :]
                                     .rearrange("e p k n -> p (e k) n")).then_inc(raw_in[raw_slot(m)], 16)
                    else:
                        c = 0 if j == 0 else j - 2
                        sp.dma_start(raw[:, raw_slot(m), :].rearrange("p (k n) -> p k n", k=KT),
                                     gu_dram[bass.ds(e_next, 1), :, :, c * UC:(c + 1) * UC]
                                     .rearrange("e p k n -> p (e k) n")).then_inc(raw_in[raw_slot(m)], 16)
            last = sp.value_load(exp_i[0:1, bass.ds(loops, 1)], min_val=0, max_val=E - 1)
            for j in range(2):
                sp.wait_ge(lo_ready, loops * 12 + (20 + 2 * j))
                m = 4 + j
                sp.dma_start(raw[:, raw_slot(m), :].rearrange("p (k n) -> p k n", k=KT // 2),
                             dn_dram[bass.ds(last, 1), :, j * 4:(j + 1) * 4, :]
                             .rearrange("e p k n -> p (e k) n")).then_inc(raw_in[raw_slot(m)], 16)
            sp.wait_ge(y_sent, loops * 16 + 32)
            for t in range(NT):
                sp.dma_start(xr[:, t, :], sum_dram[t * P:(t + 1) * P, :]).then_inc(fin_in[t], 16)
            for t in range(NT):
                sp.wait_ge(fin_out, t + 1)
                sp.dma_start(out_rows[:, t, :], xr[:, t, :]).then_inc(out_sent, 16)
            sp.wait_ge(rows_out, 16 * NT)
            sp.wait_ge(out_sent, 16 * NT)

        @block.gpsimd
        def _(pool):
            for i, g in enumerate((attn_norm_g, mem_norm_g, ffn_norm_g)):
                pool.dma_start(gains[:, i * KT:(i + 1) * KT], g.rearrange("o (k p) -> p (o k)", p=P),
                               allow_slow_non_contiguous=True).then_inc(gains_in, 16)
            pool.dma_start(g_mix, diff_subln_g.rearrange("o p -> p o"),
                           allow_slow_non_contiguous=True).then_inc(gains_in, 16)
            pool.dma_start(lam_in, diff_lambda_qk.to_broadcast([P, 4, DH])).then_inc(lam_in_s, 16)
            pool.wait_ge(exp_done, NR)
            pool.dma_start(w_rt, w_router[0].rearrange("(k p) e -> p k e", p=P)).then_inc(router_in, 16)
            pool.dma_start(br_row, b_router).then_inc(router_in, 16)
            pool.wait_ge(normed, 6 + NT)
            pool.wait_ge(x1_sent, 16)
            pool.dma_start(sum_dram[S:ROWS, :], xn[:, 0, :]).then_inc(y_sent, 16)
            for i in range(2):
                pool.dma_start(F[i * E:(i + 1) * E, 0:2 * FF], b_gate_up[0]).then_inc(bias_in_s, 16)
                pool.dma_start(F[i * E:(i + 1) * E, 2 * FF:3 * FF], b_down[0]).then_inc(bias_in_s, 16)
            pool.wait_ge(tab_ready, 1)
            pool.wait_ge(rows_out, 16 * NT)
            pool.dma_start(g_final, final_norm_g.unsqueeze(0).to_broadcast([P, D])).then_inc(gf_in, 16)
            loops = pool.value_load(loops_i[0:1, :], min_val=E - 1, max_val=MAX_LOOPS)

            def gather(column, n):
                n = n if isinstance(n, int) else pool.snap(n)
                pool.tensor_copy(idx_gather, tok_i[:, column]).then_inc(idx_ready, 1)
                pool.wait_ge(idx_ready, n)
                pool.sem_inc(gather_go, 1)
                pool.indirect_dma_start(h_row, None, h_dram,
                                        bass.IndirectOffsetOnAxis(idx_gather, 0)).then_inc(h_in, 16)

            gather(slice(0, 1), 1)
            pool.wait_ge(xtp_done, 1)
            gather(slice(1, 2), 2)

            def scatter(b, n_idx):
                copied, rows, sent = pool.snap(n_idx), pool.snap(b + 2), pool.snap(b * 16 + 16)
                pool.wait_ge(y_sent, sent)
                pool.tensor_copy(idx_scatter, sum_row_i[:, bass.ds(b, 1)]).then_inc(idx_ready, 1)
                pool.wait_ge(idx_ready, copied)
                pool.wait_ge(y_free, rows)
                pool.sem_inc(scatter_go, 1)
                pool.indirect_dma_start(sum_dram, bass.IndirectOffsetOnAxis(idx_scatter, 0),
                                        y_row, None, compute_op=ALU.add).then_inc(y_sent, 16)

            with pool.Fori(0, loops) as b:
                pool.wait_ge(xtp_done, b + 2)
                gather(bass.ds(b + 2, 1), b * 2 + 3)
                scatter(b, b * 2 + 4)
            scatter(loops, loops * 2 + 3)
            pool.wait_ge(y_sent, loops * 16 + 32)
            pool.wait_ge(h_in, loops * 16 + 32)

        @block.scalar
        def _(a):
            def hi(half, slot, raw_ap, raw_sem, value):
                a.wait_ge(raw_sem, value)
                if not isinstance(half, int) or half >= 4:
                    a.wait_ge(half_used, half - 3)
                a.activation(w_hi[:, slot, :], raw_ap, ACT.Copy).then_inc(hi_ready, 1)

            def hi_a(half):
                u = half // 2
                hi(half, half % 4, raw[:, u % 2, half % 2 * HALF:(half % 2 + 1) * HALF],
                   raw_in[u % 2], 16 * (u // 2 + 1))

            def hi_m(m, h, b=None):
                half = 16 + 2 * m + h
                value = raw_value(m)
                hi(half if b is None else b * 12 + half, half % 4,
                   raw[:, raw_slot(m), h * HALF:(h + 1) * HALF], raw_in[raw_slot(m)],
                   value if b is None else b * 32 + value)

            def mean_square(src, col):
                a.activation(junk, src, ACT.Square, scale=1.0 / math.sqrt(D),
                             accum_out=nrm[:, 0, col:col + 1]).then_inc(squares, 1)

            a.wait_ge(mem_in, 16)
            for t in range(2):
                if t:
                    a.wait_ge(squares, t)
                mean_square(mr[:, t, :], t)
            hi_a(0)
            hi_a(1)
            a.wait_ge(gains_in, 64)
            for k in range(KT):
                a.wait_ge(turn_in, k + 1)
                a.activation(act_hi[:, k, 0:MEM], psum[k][:, 0:MEM], ACT.Copy,
                             scale=g_mem[:, k:k + 1]).then_inc(turn_hi, 1)
            a.wait_ge(x_in, 16)
            a.wait_ge(normed, 2)
            for t in range(NT):
                a.wait_ge(squares, 2 + t)
                mean_square(xr[:, t, :], t)
            a.wait_ge(lam_dots, 1)
            a.activation(lamw[:, 2:4], lamw[:, 0:2], ACT.Exp).then_inc(lam_exp, 1)
            hi_a(2)
            hi_a(3)

            def proj_evac(n, dst, width):
                wait_tile(a, n)
                a.activation(dst, psum[proj_bank(n)][:, 0:width], ACT.Copy).then_inc(proj_out, 1)

            for j in range(2):
                proj_evac(j, mem_k[:, j, :], MEM)
            for t in range(2):
                proj_evac(2 + t, mem_v[:, t, :], MEM)
            for k in range(KT):
                a.wait_ge(turn_in, KT + k + 1)
                a.activation(act_hi[:, k, :], psum[k][:, :], ACT.Copy,
                             scale=g_attn[:, k:k + 1]).then_inc(turn_hi, 1)
            n = 4
            for u in range(1, 6):
                hi_a(2 * u + 2)
                hi_a(2 * u + 3)
                if u in (1, 2, 4):
                    first = {1: 0, 2: 4, 4: 8}[u]
                    dsts = [(qk[:, first + i, :], S) for i in range(4)]
                elif u == 3:
                    dsts = [(diff_v[:, t, :], 512) for t in range(NT)]
                else:
                    dsts = [(dil_v[:, t, :], 256) for t in range(NT)] + [(qk[:, 12 + i, :], S) for i in range(2)]
                for dst, width in dsts:
                    proj_evac(n, dst, width)
                    n += 1
            hi_a(14)
            hi_a(15)

            for i in range(STEPS):
                t = task(i - LAG_T)
                if t is not None:
                    ti = turned[t]
                    a.wait_ge(pt_in, ti + 1)
                    if t[0] == "mix":
                        src = psum[4 + ti % 2][:, :].rearrange("p (k s) -> p k s", k=4)
                        dst = act_hi[:, 4 * t[1]:4 * t[1] + 4, t[2] * P:(t[2] + 1) * P]
                        a.activation(dst, src, ACT.Copy,
                                     scale=g_mix if t[1] == 0 else 1.0).then_inc(pt_out, 1)
                    else:
                        r = real[t]
                        if r >= 2:
                            a.wait_ge(pv_done, r - 1)
                        n = n_keys(t)
                        a.activation(pt[:, r % 2, 0:n], psum[4 + ti % 2][:, 0:n], ACT.Copy).then_inc(pt_out, 1)
                t = task(i)
                if is_real(t):
                    r = real[t]
                    st = stat[:, r % 8, :]
                    n = n_keys(t)
                    a.wait_ge(max_done, r + 1)
                    if t[0] == "mem":
                        if r >= 2:
                            a.wait_ge(pt_in, turned_index(r - 2) + 1)
                        a.activation(probs[:, r % 2, 0, 0:n], psum[2 * (r % 2)][:, 0:n], ACT.Exp,
                                     bias=st[:, 2:3], scale=SCALE, accum_out=st[:, 4:5]).then_inc(exp_done, 1)
                    else:
                        branches = 2 if t[0] == "diff" else 1
                        for j in range(branches):
                            ins = a.activation(probs[:, r % 2, j, 0:n], probs[:, r % 2, j, 0:n], ACT.Exp,
                                               bias=st[:, 2 + j:3 + j], accum_out=st[:, 4 + j:5 + j])
                        ins.then_inc(exp_done, 1)

            hi_m(0, 0)
            hi_m(0, 1)
            for t in range(NT):
                a.wait_ge(wo_done, NT + t + 1)
                a.wait_ge(squares, 6 + t)
                mean_square(xr[:, t, :], t)
            hi_m(1, 0)
            hi_m(1, 1)
            for t in range(NT):
                for q in range(2):
                    i = 2 * t + q
                    a.wait_ge(ht_in, i + 1)
                    if t >= 2:
                        a.wait_ge(lg_in, t - 1)
                    a.activation(hT[:, t % 2, 4 * q:4 * q + 4, :],
                                 psum[i % 4][:, :].rearrange("p (k s) -> p k s", k=4), ACT.Copy).then_inc(ht_out, 1)
            a.wait_ge(top_ready, 1)
            for t in range(NT):
                a.activation(gate_e[:, t, :], top[:, t, 0:TOPK], ACT.Exp, bias=ntop[:, t:t + 1],
                             accum_out=gate_s[:, t:t + 1]).then_inc(gates_e, 1)

            def turn_x(q, n):
                a.wait_ge(xtp_done, n)
                bank = psum[6 + q][:, :].rearrange("p (k s) -> p k s", k=4)
                for k in range(4):
                    ins = a.activation(hx[:, 4 * q + k, :], bank[:, k, :], ACT.Copy,
                                       scale=g_ffn[:, 4 * q + k:4 * q + k + 1])
                ins.then_inc(xhi_ready, 1)

            def turn_act(q, n):
                a.wait_ge(atp_done, n)
                a.activation(ha[:, 4 * q:4 * q + 4, :],
                             psum[6 + q][:, :].rearrange("p (k s) -> p k s", k=4), ACT.Copy).then_inc(ahi_ready, 1)

            def sigmoid(c, n):
                a.wait_ge(gate_ready, n)
                a.activation(sig_c[:, c % 2, :], gate_c[:, c % 2, :], ACT.Sigmoid,
                             scale=ALPHA).then_inc(sig_ready, 1)

            def y_out(used, column, sent):
                a.wait_ge(half_used, used)
                a.wait_ge(y_sent, sent)
                for c in range(2):
                    ins = a.activation(y_row[:, c * 512:(c + 1) * 512], psum[4 + c][:, :], ACT.Copy,
                                       scale=gate_t[:, column])
                ins.then_inc(y_free, 1)

            a.wait_ge(tab_ready, 1)
            a.sem_inc(y_free, 1)
            loops = a.value_load(loops_i[0:1, :], min_val=E - 1, max_val=MAX_LOOPS)
            turn_x(0, 1)
            turn_x(1, 1)
            sigmoid(0, 1)
            with a.Fori(0, loops) as b:
                hi_m(2, 0, b)
                hi_m(2, 1, b)
                hi_m(3, 0, b)
                hi_m(3, 1, b)
                sigmoid(1, b * 4 + 2)
                hi_m(4, 0, b)
                hi_m(4, 1, b)
                sigmoid(2, b * 4 + 3)
                a.wait_ge(half_used, b * 12 + (16 + 2 * 3 + 1))
                turn_x(0, b + 2)
                hi_m(5, 0, b)
                a.wait_ge(half_used, b * 12 + (16 + 2 * 3 + 2))
                turn_x(1, b + 2)
                hi_m(5, 1, b)
                turn_act(0, b * 2 + 1)
                sigmoid(3, b * 4 + 4)
                hi_m(6, 0, b)
                hi_m(6, 1, b)
                turn_act(1, b * 2 + 2)
                sigmoid(0, b * 4 + 5)
                hi_m(7, 0, b)
                hi_m(7, 1, b)
                y_out(b * 12 + 30, bass.ds(b, 1), b * 16 + 16)
            b = loops
            hi_m(2, 0, b)
            hi_m(2, 1, b)
            hi_m(3, 0, b)
            hi_m(3, 1, b)
            sigmoid(1, b * 4 + 2)
            hi_m(4, 0, b)
            hi_m(4, 1, b)
            sigmoid(2, b * 4 + 3)
            hi_m(5, 0, b)
            turn_act(0, b * 2 + 1)
            sigmoid(3, b * 4 + 4)
            hi_m(5, 1, b)
            turn_act(1, b * 2 + 2)
            y_out(b * 12 + 28, bass.ds(b, 1), b * 16 + 16)
            for t in range(NT):
                a.wait_ge(fin_in[t], 16)
                a.wait_ge(squares, 10 + t)
                mean_square(xr[:, t, :], t)

        @block.vector
        def _(v):
            seq = [0]

            def link(ins):
                seq[0] += 1
                ins.then_inc(dve_seq, 1)
                v.wait_ge(dve_seq, seq[0])

            def rsqrt(n):
                ms, y, t1, t2 = (nrm[:, i, 0:n] for i in range(4))
                link(v.tensor_scalar(ms, ms, EPS, None, ALU.add))
                link(v.tensor_scalar(t1.bitcast(I32), ms.bitcast(I32), 1, None, ALU.arith_shift_right))
                link(v.tensor_scalar(y.bitcast(I32), t1.bitcast(I32), -1, 0x5F3759DF, ALU.mult, ALU.add))
                for _ in range(4):
                    link(v.scalar_tensor_tensor(out=t1, in0=y, scalar=-0.5, in1=y, op0=ALU.mult, op1=ALU.mult))
                    link(v.tensor_tensor(t2, t1, ms, ALU.mult))
                    link(v.scalar_tensor_tensor(out=y, in0=t2, scalar=1.5, in1=y, op0=ALU.add, op1=ALU.mult))

            def lo(half, slot, raw_ap):
                v.wait_ge(hi_ready, half + 1)
                v.tensor_tensor(w_lo[:, slot, :], raw_ap, w_hi[:, slot, :].bitcast(F32),
                                ALU.subtract).then_inc(lo_ready, 1)

            def lo_a(half):
                lo(half, half % 4, raw[:, half // 2 % 2, half % 2 * HALF:(half % 2 + 1) * HALF])

            def lo_m(m, h, b=None):
                half = 16 + 2 * m + h
                lo(half if b is None else b * 12 + half, half % 4,
                   raw[:, raw_slot(m), h * HALF:(h + 1) * HALF])

            v.wait_ge(squares, 2)
            rsqrt(2)
            for t in range(2):
                v.tensor_scalar(mr[:, t, :], mr[:, t, :], nrm[:, 1, t:t + 1], None, ALU.mult).then_inc(normed, 1)
            v.wait_ge(gains_in, 64)
            link(v.tensor_scalar(g_mix, g_mix, 1.0 - LAM_INIT, None, ALU.mult))
            lo_a(0)
            lo_a(1)
            for k in range(KT):
                v.wait_ge(turn_hi, k + 1)
                v.scalar_tensor_tensor(out=act_lo[:, k, 0:MEM], in0=psum[k][:, 0:MEM], scalar=g_mem[:, k:k + 1],
                                       in1=act_hi[:, k, 0:MEM].bitcast(F32), op0=ALU.mult,
                                       op1=ALU.subtract).then_inc(turn_lo, 1)
            v.wait_ge(lam_in_s, 16)
            for j in range(2):
                link(v.tensor_tensor_reduce(lam_in[:, 2 * j, :], lam_in[:, 2 * j, :], lam_in[:, 2 * j + 1, :],
                                            1.0, 0.0, ALU.mult, ALU.add, lamw[:, j:j + 1]))
            v.tensor_copy(lamw[:, 6:8], lamw[:, 0:2]).then_inc(lam_dots, 1)
            v.wait_ge(squares, 2 + NT)
            rsqrt(NT)
            for t in range(NT):
                v.tensor_scalar(xr[:, t, :], xr[:, t, :], nrm[:, 1, t:t + 1], None, ALU.mult).then_inc(normed, 1)
            lo_a(2)
            lo_a(3)
            v.wait_ge(lam_exp, 1)
            link(v.tensor_tensor(lamw[:, 4:5], lamw[:, 3:4], lamw[:, 2:3], ALU.subtract))
            link(v.tensor_scalar(lamw[:, 5:6], lamw[:, 4:5], LAM_INIT, None, ALU.subtract))
            for k in range(KT):
                v.wait_ge(turn_hi, KT + k + 1)
                v.scalar_tensor_tensor(out=act_lo[:, k, :], in0=psum[k][:, :], scalar=g_attn[:, k:k + 1],
                                       in1=act_hi[:, k, :].bitcast(F32), op0=ALU.mult,
                                       op1=ALU.subtract).then_inc(turn_lo, 1)
            for half in range(4, 16):
                lo_a(half)

            v.wait_ge(pos_in, 16)

            def soft(t):
                r = real[t]
                st = stat[:, r % 8, :]
                n = n_keys(t)
                v.wait_ge(sc_ready, r + 1)
                if t[0] == "mem":
                    link(v.tensor_reduce(st[:, 0:1], psum[2 * (r % 2)][:, 0:n], AX_X, ALU.max))
                    v.tensor_scalar(st[:, 2:3], st[:, 0:1], -SCALE, None, ALU.mult).then_inc(max_done, 1)
                    return
                if r >= 2:
                    v.wait_ge(pt_in, turned_index(r - 2) + 1)
                branches = 2 if t[0] == "diff" else 1
                table = t[1] if t[0] == "diff" else HEADS + t[1]
                for j in range(branches):
                    link(v.tensor_tensor_reduce(probs[:, r % 2, j, 0:n], psum[2 * (r % 2) + j][:, 0:n],
                                                pos[:, table, S - n:S], SCALE, NEG, ALU.add, ALU.max,
                                                st[:, j:j + 1]))
                v.tensor_scalar(st[:, 2:2 + branches], st[:, 0:branches], -1.0, None,
                                ALU.mult).then_inc(max_done, 1)

            def combine(t):
                r = real[t]
                st = stat[:, r % 8, :]
                n = n_keys(t)
                v.wait_ge(exp_done, r + 1)
                if t[0] != "diff":
                    v.reciprocal(st[:, 6:7], st[:, 4:5]).then_inc(prob_ready, 1)
                    return
                link(v.reciprocal(st[:, 6:8], st[:, 4:6]))
                link(v.tensor_scalar(st[:, 7:8], st[:, 7:8], lamw[:, 5:6], None, ALU.mult))
                p1, p2 = probs[:, r % 2, 0, 0:n], probs[:, r % 2, 1, 0:n]
                link(v.tensor_scalar(p1, p1, st[:, 6:7], None, ALU.mult))
                v.scalar_tensor_tensor(out=p1, in0=p2, scalar=st[:, 7:8], in1=p1, op0=ALU.mult,
                                       op1=ALU.add).then_inc(prob_ready, 1)

            mixes = [0]

            def finish(t):
                if t[0] == "mix":
                    ti = turned[t]
                    mixes[0] += 1
                    v.wait_ge(pt_out, ti + 1)
                    src = psum[4 + ti % 2][:, :].rearrange("p (k s) -> p k s", k=4)
                    part = (slice(None), slice(4 * t[1], 4 * t[1] + 4), slice(t[2] * P, (t[2] + 1) * P))
                    v.scalar_tensor_tensor(out=act_lo[part], in0=src, scalar=g_mix if t[1] == 0 else 1.0,
                                           in1=act_hi[part].bitcast(F32), op0=ALU.mult,
                                           op1=ALU.subtract).then_inc(mix_lo, 1)
                    return
                kind, h, qb = t
                r = real[t]
                o = psum[6 + r % 2]
                v.wait_ge(pv_done, r + 1)
                if kind != "diff":
                    at0 = 512 + 256 * (kind == "mem") + h * DH
                    v.tensor_scalar(mix[:, at0:at0 + DH], o[:, 0:DH], stat[:, r % 8, 6:7], None,
                                    ALU.mult).then_inc(out_done, 1)
                    return
                if h == 0 and qb:
                    v.wait_ge(pt_in, turned[("mix", 1, qb - 1)] + 1)
                mine = mix[:, h * P:(h + 1) * P]
                link(v.tensor_copy(mine, o[:, 0:P]))
                ins = v.tensor_tensor_reduce(o[:, 256:256 + P], mine, mine, 1.0 / P, 0.0, ALU.mult, ALU.add,
                                             nrm[:, 0, h:h + 1])
                if h < HEADS - 1:
                    ins.then_inc(out_done, 1)
                    return
                link(ins)
                rsqrt(HEADS)
                for g in range(HEADS):
                    ins = v.tensor_scalar(mix[:, g * P:(g + 1) * P], mix[:, g * P:(g + 1) * P],
                                          nrm[:, 1, g:g + 1], None, ALU.mult)
                ins.then_inc(out_done, 1)

            for i in range(STEPS):
                if is_real(task(i)):
                    soft(task(i))
                if is_real(task(i - 1)):
                    combine(task(i - 1))
                if task(i - LAG_V) is not None:
                    finish(task(i - LAG_V))

            v.wait_ge(x_again, 16)
            for n in range(2 * NT):
                c, t = n // NT, n % NT
                wait_tile(v, N_IN + n)
                half_row = xr[:, t, c * 512:(c + 1) * 512]
                v.tensor_tensor(half_row, psum[n][:, :], half_row, ALU.add).then_inc(wo_done, 1)
                if n == 5:
                    lo_m(0, 0)
                    lo_m(0, 1)
            v.wait_ge(router_in, 32)
            v.tensor_tensor(w_rt, w_rt, g_ffn.unsqueeze(2).to_broadcast([P, KT, E]), ALU.mult).then_inc(router_g, 1)
            v.wait_ge(squares, 6 + NT)
            rsqrt(NT)
            for t in range(NT):
                v.tensor_scalar(xn[:, t, :], xr[:, t, :], nrm[:, 1, t:t + 1], None, ALU.mult).then_inc(normed, 1)
            lo_m(1, 0)
            lo_m(1, 1)

            for t in range(NT):
                v.wait_ge(lg_in, t + 1)
                link(v.tensor_copy(lg[:, t, :], psum[4 + t][:, 0:E]))
                link(v.max(top[:, t, :], lg[:, t, :]))
                link(v.max_index(top_i[:, t, :], top[:, t, :], lg[:, t, :]))
            v.tensor_scalar(ntop, top[:, :, 0], -1.0, None, ALU.mult).then_inc(top_ready, 1)
            link(v.tensor_copy(top_f, top_i))
            link(v.tensor_tensor(picked, iota[:, 0:E].unsqueeze(1).unsqueeze(1).to_broadcast([P, NT, TOPK, E]),
                                 top_f[:, :, 0:TOPK].unsqueeze(3).to_broadcast([P, NT, TOPK, E]), ALU.is_equal))
            link(v.tensor_tensor(chosen, picked[:, :, 0, :], picked[:, :, 1, :], ALU.add))
            link(v.tensor_tensor(chosen, chosen, picked[:, :, 2, :], ALU.add))
            v.tensor_tensor(chosen, chosen, picked[:, :, 3, :], ALU.add).then_inc(chosen_ready, 1)
            link(v.memset(cum, 0.0))
            v.wait_ge(rank_in, 1)
            count = psum[0][:, NT * E:(NT + 1) * E]
            link(v.tensor_scalar(n_blk, count, float(P), 1.0, ALU.is_gt, ALU.add))
            for j in (2, 3):
                link(v.scalar_tensor_tensor(out=n_blk, in0=count, scalar=float(P * j), in1=n_blk,
                                            op0=ALU.is_gt, op1=ALU.add))
            link(v.tensor_copy(cum[:, 0, E:2 * E], n_blk))
            cur = 0
            for shift in (1, 2, 4, 8, 16):
                link(v.tensor_tensor(cum[:, 1 - cur, E:2 * E], cum[:, cur, E:2 * E],
                                     cum[:, cur, E - shift:2 * E - shift], ALU.add))
                cur = 1 - cur
            b_end = cum[:, cur, E:2 * E]
            link(v.tensor_tensor(b_start, b_end, n_blk, ALU.subtract))
            for t in range(NT):
                link(v.scalar_tensor_tensor(out=slots[:, t, :], in0=b_start, scalar=float(P),
                                            in1=psum[0][:, t * E:(t + 1) * E], op0=ALU.mult, op1=ALU.add))
            for t in range(NT):
                for k in range(TOPK):
                    link(v.tensor_tensor_reduce(cum[:, 1 - cur, 0:E], picked[:, t, k, :], slots[:, t, :], 1.0, 0.0,
                                                ALU.mult, ALU.add, slot_f[:, t * TOPK + k:t * TOPK + k + 1]))
            link(v.tensor_copy(slot_i, slot_f))
            link(v.tensor_scalar(loc_i, slot_i, P - 1, None, ALU.bitwise_and))
            link(v.tensor_scalar(blk_i, slot_i, 7, None, ALU.arith_shift_right))
            link(v.tensor_copy(loc_f, loc_i))
            link(v.tensor_copy(blk_f, blk_i))
            v.wait_ge(gates_e, NT)
            link(v.reciprocal(gate_s, gate_s))
            for t in range(NT):
                link(v.tensor_scalar(gate_e[:, t, :], gate_e[:, t, :], gate_s[:, t:t + 1], None, ALU.mult))
            v.wait_ge(ht_out, 2 * NT)
            v.wait_ge(lg_in, NT)
            blocks = iota[:, 0:MAX_BLOCKS]
            link(v.tensor_tensor(e_cmp, blocks.unsqueeze(2).to_broadcast([P, MAX_BLOCKS, E]),
                                 b_end.unsqueeze(1).to_broadcast([P, MAX_BLOCKS, E]), ALU.is_ge))
            link(v.tensor_reduce(exp_f, e_cmp, AX_X, ALU.add))
            link(v.tensor_scalar(exp_f, exp_f, float(E - 1), None, ALU.min))
            link(v.tensor_copy(exp_i, exp_f))
            link(v.tensor_scalar(n_blk[:, 0:1], b_end[:, E - 1:E], 1.0, None, ALU.subtract))
            link(v.tensor_copy(loops_i, n_blk[:, 0:1]))
            for t in range(NT):
                for k in range(TOPK):
                    i = t * TOPK + k
                    v.tensor_scalar(lane_hot[:, i, :], iota, loc_f[:, i:i + 1], None, ALU.is_equal)
                    v.tensor_scalar(blk_hot[:, i, 0, :], blocks, blk_f[:, i:i + 1],
                                    cst[:, C_TOK + t:C_TOK + t + 1], ALU.is_equal, ALU.mult)
                    v.tensor_scalar(blk_hot[:, i, 1, :], blocks, blk_f[:, i:i + 1],
                                    gate_e[:, t, k:k + 1], ALU.is_equal, ALU.mult).then_inc(hot_ready, 1)
            v.wait_ge(bias_in_s, 64)
            v.wait_ge(half_used, 16)
            v.memset(R[2 * E:P, 4 * D:7 * D].bitcast(F32), 0.0)
            link(v.tensor_copy(bias[0:2 * E, :], bias_in))
            v.tensor_tensor(bias[E:2 * E, :], bias_in[E:2 * E, :], bias[E:2 * E, :].bitcast(F32),
                            ALU.subtract).then_inc(bias_ready, 1)
            v.wait_ge(tab_in, 1)
            link(v.tensor_copy(tok_f, psum[1][:, 0:MAX_BLOCKS]))
            link(v.tensor_copy(gate_t, psum[1][:, MAX_BLOCKS:2 * MAX_BLOCKS]))
            link(v.tensor_scalar(idle_f, tok_f, 0.0, cst[:, C_IDLE:C_IDLE + 1], ALU.is_equal, ALU.mult))
            link(v.scalar_tensor_tensor(out=tok_f, in0=tok_f, scalar=-1.0, in1=idle_f, op0=ALU.add, op1=ALU.add))
            link(v.tensor_copy(sum_row_i, tok_f))
            link(v.tensor_scalar(tok_f, tok_f, float(S - 1), None, ALU.min))
            v.tensor_copy(tok_i, tok_f).then_inc(tab_ready, 1)
            v.wait_ge(tab_ready, 1)

            def turn_x(q, n):
                v.wait_ge(xhi_ready, n)
                bank = psum[6 + q][:, :].rearrange("p (k s) -> p k s", k=4)
                for k in range(4):
                    kk = 4 * q + k
                    ins = v.scalar_tensor_tensor(out=lx[:, kk, :], in0=bank[:, k, :], scalar=g_ffn[:, kk:kk + 1],
                                                 in1=hx[:, kk, :].bitcast(F32), op0=ALU.mult, op1=ALU.subtract)
                ins.then_inc(xlo_ready, 1)

            def turn_act(q, n):
                v.wait_ge(ahi_ready, n)
                v.tensor_tensor(la[:, 4 * q:4 * q + 4, :], psum[6 + q][:, :].rearrange("p (k s) -> p k s", k=4),
                                ha[:, 4 * q:4 * q + 4, :].bitcast(F32), ALU.subtract).then_inc(alo_ready, 1)

            def choose(column):
                v.tensor_scalar(pick, cst[:, C_ROWMOD:C_ROWMOD + 1].to_broadcast([P, P]), exp_f[:, column], None,
                                ALU.is_equal).then_inc(pick_ready, 1)

            def clamp(c, n):
                v.wait_ge(gu_done, n)
                pairs = psum[c][:, :].rearrange("p (i two) -> p two i", two=2)
                v.tensor_scalar(gate_c[:, c % 2, :], pairs[:, 0, :], LIMIT, None, ALU.min).then_inc(gate_ready, 1)
                v.tensor_scalar(up_c[:, c % 2, :], pairs[:, 1, :], LIMIT, -LIMIT, ALU.min,
                                ALU.max).then_inc(gu_free, 1)
                v.wait_ge(gu_free, n + 4)
                v.scalar_tensor_tensor(out=prod_c[:, c % 2, :], in0=up_c[:, c % 2, :], scalar=1.0,
                                       in1=gate_c[:, c % 2, :], op0=ALU.add, op1=ALU.mult).then_inc(prod_ready, 1)

            def activate(c, n):
                v.wait_ge(sig_ready, n)
                v.wait_ge(prod_ready, n)
                v.tensor_tensor(act[:, c * 256:(c + 1) * 256], prod_c[:, c % 2, :], sig_c[:, c % 2, :],
                                ALU.mult).then_inc(act_ready, 1)

            v.sem_inc(gu_free, 4)
            choose(slice(0, 1))
            turn_x(0, 1)
            turn_x(1, 2)
            clamp(0, 1)
            loops = v.value_load(loops_i[0:1, :], min_val=E - 1, max_val=MAX_LOOPS)
            with v.Fori(0, loops) as b:
                lo_m(2, 0, b)
                activate(0, b * 4 + 1)
                lo_m(2, 1, b)
                lo_m(3, 0, b)
                lo_m(3, 1, b)
                clamp(1, b * 4 + 2)
                lo_m(4, 0, b)
                activate(1, b * 4 + 2)
                lo_m(4, 1, b)
                clamp(2, b * 4 + 3)
                turn_x(0, b * 2 + 3)
                lo_m(5, 0, b)
                activate(2, b * 4 + 3)
                v.wait_ge(ybias_done, b + 1)
                choose(bass.ds(b + 1, 1))
                turn_x(1, b * 2 + 4)
                lo_m(5, 1, b)
                turn_act(0, b * 2 + 1)
                clamp(3, b * 4 + 4)
                lo_m(6, 0, b)
                activate(3, b * 4 + 4)
                lo_m(6, 1, b)
                turn_act(1, b * 2 + 2)
                clamp(0, b * 4 + 5)
                lo_m(7, 0, b)
                lo_m(7, 1, b)
            b = loops
            lo_m(2, 0, b)
            activate(0, b * 4 + 1)
            lo_m(2, 1, b)
            lo_m(3, 0, b)
            lo_m(3, 1, b)
            clamp(1, b * 4 + 2)
            lo_m(4, 0, b)
            activate(1, b * 4 + 2)
            lo_m(4, 1, b)
            clamp(2, b * 4 + 3)
            lo_m(5, 0, b)
            activate(2, b * 4 + 3)
            turn_act(0, b * 2 + 1)
            clamp(3, b * 4 + 4)
            activate(3, b * 4 + 4)
            lo_m(5, 1, b)
            turn_act(1, b * 2 + 2)

            v.wait_ge(gf_in, 16)
            v.wait_ge(squares, 10 + NT)
            rsqrt(NT)
            for t in range(NT):
                v.scalar_tensor_tensor(out=xr[:, t, :], in0=xr[:, t, :], scalar=nrm[:, 1, t:t + 1], in1=g_final,
                                       op0=ALU.mult, op1=ALU.mult).then_inc(fin_out, 1)

        @block.tensor
        def _(pe):
            def three(bank, a, b, first=False, last=False):
                pe.matmul(bank, a[0], b[0], start=first, stop=False)
                pe.matmul(bank, a[0], b[1], start=False, stop=False)
                return pe.matmul(bank, a[1], b[0], start=False, stop=last)

            def w_part(slot, c0, c1):
                return w_hi[:, slot, c0:c1], w_lo[:, slot, c0:c1]

            def project(n):
                u, width, turned_out, c0, s0, is_last = TILES[n]
                bank = psum[proj_bank(n)][:, 0:width]
                for k in range(KT):
                    half = 2 * u + k // 4
                    at0 = k % 4 * UC + c0
                    if k % 4 == 0:
                        pe.wait_ge(lo_ready, half + 1)
                    if turned_out:
                        ins = three(bank, w_part(half % 4, at0, at0 + P),
                                    (act_hi[:, k, s0:s0 + width], act_lo[:, k, s0:s0 + width]), k == 0, k == KT - 1)
                    else:
                        ins = three(bank, (act_hi[:, k, s0:s0 + P], act_lo[:, k, s0:s0 + P]),
                                    w_part(half % 4, at0, at0 + width), k == 0, k == KT - 1)
                    if is_last and k == 3:
                        ins.then_inc(half_used, 1)
                ins.then_inc(half_used if is_last else proj_in, 1)

            pe.wait_ge(const_in, 16)
            pe.wait_ge(normed, 2)
            for k in range(KT):
                for t in range(2):
                    ins = pe.transpose(psum[k][:, t * P:(t + 1) * P], mr[:, t, k * P:(k + 1) * P], ident)
                ins.then_inc(turn_in, 1)
            pe.wait_ge(turn_lo, KT)
            for n in range(4):
                project(n)
            pe.wait_ge(normed, 6)
            pe.wait_ge(proj_out, 4)
            for k in range(KT):
                for t in range(NT):
                    ins = pe.transpose(psum[k][:, t * P:(t + 1) * P], xr[:, t, k * P:(k + 1) * P], ident)
                ins.then_inc(turn_in, 1)
            pe.wait_ge(turn_lo, 2 * KT)
            for n in range(4, N_IN):
                if n >= 8:
                    pe.wait_ge(proj_out, n - 3)
                project(n)

            pe.wait_ge(proj_out, N_IN)
            for i in range(STEPS):
                t = task(i)
                if is_real(t):
                    kind, h, qb = t
                    r = real[t]
                    n = n_keys(t)
                    if r >= 2:
                        pe.wait_ge(exp_done, r - 1)
                    q0 = qb * P
                    if kind == "diff":
                        for j in range(2):
                            rows = slice(j * DH, (j + 1) * DH)
                            ins = pe.matmul(psum[2 * (r % 2) + j][:, 0:n], qk[rows, h, q0:q0 + P],
                                            qk[rows, 4 + h, 0:n], start=True, stop=True)
                    else:
                        rows = slice(h % 2 * DH, (h % 2 + 1) * DH)
                        q_tile, keys = (8, qk[rows, 10 + h // 2, 0:n]) if kind == "dil" \
                            else (12, mem_k[rows, h // 2, :])
                        ins = pe.matmul(psum[2 * (r % 2)][:, 0:n], qk[rows, q_tile + h // 2, q0:q0 + P], keys,
                                        start=True, stop=True)
                    ins.then_inc(sc_ready, 1)
                t = task(i - LAG_T)
                if t is not None:
                    ti = turned[t]
                    if ti >= 2:
                        before = by_turn[ti - 2]
                        if before[0] == "mix":
                            pe.wait_ge(mix_lo, 2 * before[2] + before[1] + 1)
                        else:
                            pe.wait_ge(pt_out, ti - 1)
                    if t[0] == "mix":
                        last_head = ("diff", HEADS - 1, t[2]) if t[1] == 0 else ("mem", HEADS - 1, t[2])
                        pe.wait_ge(out_done, real[last_head] + 1)
                        for k in range(4):
                            c0 = (4 * t[1] + k) * P
                            ins = pe.transpose(psum[4 + ti % 2][:, k * P:(k + 1) * P], mix[:, c0:c0 + P], ident)
                    else:
                        r = real[t]
                        pe.wait_ge(prob_ready, r + 1)
                        for kb in range(n_keys(t) // P):
                            ins = pe.transpose(psum[4 + ti % 2][:, kb * P:(kb + 1) * P],
                                               probs[:, r % 2, 0, kb * P:(kb + 1) * P], ident)
                    ins.then_inc(pt_in, 1)
                t = task(i - LAG_V)
                if is_real(t):
                    kind, h, qb = t
                    r = real[t]
                    pe.wait_ge(pt_out, turned[t] + 1)
                    if r >= 2:
                        pe.wait_ge(out_done, r - 1)
                    nb = n_keys(t) // P
                    for kb in range(nb):
                        values = {"diff": diff_v[:, kb, h * P:(h + 1) * P],
                                  "dil": dil_v[:, kb, h * DH:(h + 1) * DH],
                                  "mem": mem_v[:, kb % 2, h * DH:(h + 1) * DH]}[kind]
                        ins = pe.matmul(psum[6 + r % 2][:, 0:P if kind == "diff" else DH],
                                        pt[:, r % 2, kb * P:(kb + 1) * P], values,
                                        start=kb == 0, stop=kb == nb - 1)
                    ins.then_inc(pv_done, 1)

            pe.wait_ge(mix_lo, 2 * NT)
            pe.wait_ge(exp_done, NR)
            pe.wait_ge(out_done, NR)
            for n in range(N_IN, len(TILES)):
                project(n)

            pe.wait_ge(router_in, 32)
            pe.wait_ge(router_g, 1)
            for t in range(NT):
                pe.wait_ge(normed, 6 + t + 1)
                for q in range(2):
                    i = 2 * t + q
                    if i >= 4:
                        pe.wait_ge(ht_out, i - 3)
                    for k in range(4):
                        ins = pe.transpose(psum[i % 4][:, k * P:(k + 1) * P],
                                           xn[:, t, (4 * q + k) * P:(4 * q + k + 1) * P], ident)
                    ins.then_inc(ht_in, 1)
                pe.wait_ge(ht_out, 2 * t + 2)
                for k in range(KT):
                    pe.matmul(psum[4 + t][:, 0:E], hT[:, t % 2, k, :], w_rt[:, k, :], start=k == 0, stop=False)
                pe.matmul(psum[4 + t][:, 0:E], ones[0:1, :], br_row, start=False, stop=True).then_inc(lg_in, 1)
            pe.wait_ge(chosen_ready, 1)
            for t in range(NT):
                bank = psum[0][:, t * E:(t + 1) * E]
                for before in range(t):
                    pe.matmul(bank, ones, chosen[:, before, :], start=before == 0, stop=False)
                pe.matmul(bank, tri, chosen[:, t, :], start=t == 0, stop=True)
            for t in range(NT):
                ins = pe.matmul(psum[0][:, NT * E:(NT + 1) * E], ones, chosen[:, t, :], start=t == 0, stop=t == NT - 1)
            ins.then_inc(rank_in, 1)
            for i in range(NT * TOPK):
                pe.wait_ge(hot_ready, i + 1)
                ins = pe.matmul(psum[1][:, 0:2 * MAX_BLOCKS], lane_hot[:, i, :],
                                blk_hot[:, i, :, :].rearrange("p j b -> p (j b)"),
                                start=i == 0, stop=i == NT * TOPK - 1)
            ins.then_inc(tab_in, 1)

            def half_in(m, h, b):
                half = 16 + 2 * m + h
                pe.wait_ge(lo_ready, half + 1 if b is None else b * 12 + (half + 1))
                return half % 4

            def gate_up(m, c, b, n_free, rows=None, n_pick=None):
                pe.wait_ge(gu_free, n_free)
                for h in range(2):
                    slot = half_in(m, h, b)
                    if rows is not None:
                        pe.wait_ge(xlo_ready, rows[h])
                    for kk in range(4):
                        k = 4 * h + kk
                        ins = three(psum[c][:, :], (hx[:, k, :], lx[:, k, :]), w_part(slot, kk * UC, (kk + 1) * UC),
                                    first=k == 0)
                    ins.then_inc(half_used, 1)
                    if h == 0 and c == 0 and b is not None:
                        turn_acts(0, b * 4 + 2)
                if n_pick is not None:
                    pe.wait_ge(pick_ready, n_pick)
                pe.matmul(psum[c][:, :], pick, bias[:, c * 512:(c + 1) * 512], start=False,
                          stop=True).then_inc(gu_done, 1)

            def turn_rows(n_h):
                pe.wait_ge(h_in, n_h)
                for k in range(KT):
                    ins = pe.transpose(psum[6 + k // 4][:, k % 4 * P:(k % 4 + 1) * P],
                                       h_row[:, k * P:(k + 1) * P], ident)
                ins.then_inc(xtp_done, 1)

            def turn_acts(q, n):
                pe.wait_ge(act_ready, n)
                for k in range(4):
                    c0 = (4 * q + k) * P
                    ins = pe.transpose(psum[6 + q][:, k * P:(k + 1) * P], act[:, c0:c0 + P], ident)
                ins.then_inc(atp_done, 1)

            def y_bias(b):
                pe.wait_ge(y_free, b + 1)
                for c in range(2):
                    ins = pe.matmul(psum[4 + c][:, :], pick, bias[:, 2 * FF + c * 512:2 * FF + (c + 1) * 512],
                                    start=True, stop=False)
                ins.then_inc(ybias_done, 1)

            def down(m, b):
                for u in range(2):
                    pe.wait_ge(alo_ready, b * 2 + (u + 1))
                    for h in range(2):
                        slot = half_in(m + u, h, b)
                        for kk in range(2):
                            k = 4 * u + 2 * h + kk
                            for c in range(2):
                                at0 = kk * D + c * 512
                                ins = three(psum[4 + c][:, :], (ha[:, k, :], la[:, k, :]),
                                            w_part(slot, at0, at0 + 512), last=k == KT - 1)
                        ins.then_inc(half_used, 1)
                        if u == 0 and h == 0:
                            turn_acts(1, b * 4 + 4)

            turn_rows(16)
            pe.wait_ge(bias_ready, 1)
            gate_up(0, 0, None, 1, rows=(1, 2), n_pick=1)
            pe.wait_ge(tab_ready, 1)
            loops = pe.value_load(loops_i[0:1, :], min_val=E - 1, max_val=MAX_LOOPS)
            with pe.Fori(0, loops) as b:
                gate_up(1, 1, b, b * 4 + 2)
                turn_rows(b * 16 + 32)
                gate_up(2, 2, b, b * 4 + 3)
                gate_up(3, 3, b, b * 4 + 4)
                y_bias(b)
                gate_up(4, 0, b, b * 4 + 5, rows=(b * 2 + 3, b * 2 + 4), n_pick=b + 2)
                down(5, b)
            b = loops
            gate_up(1, 1, b, b * 4 + 2)
            gate_up(2, 2, b, b * 4 + 3)
            gate_up(3, 3, b, b * 4 + 4)
            y_bias(b)
            turn_acts(0, b * 4 + 2)
            down(4, b)


_INS = ["x", "mem", "attn_norm_g", "mem_norm_g", "w_in", "diff_lambda_qk", "diff_subln_g", "w_mem_kv", "w_out",
        "ffn_norm_g", "w_router", "b_router", "w_gate_up", "b_gate_up", "w_down", "b_down", "final_norm_g"]


def kernel(**inputs):
    import concourse.bacc as bacc
    from concourse.bass_utils import run_bass_kernel_spmd

    nc = bacc.Bacc("TRN2", target_bir_lowering=False, num_devices=1)
    given = {name: np.ascontiguousarray(inputs[name]) for name in _INS}
    given["constants"] = constants()
    given["position_tables"] = position_tables()
    arrays, args = {}, []
    for name, a in given.items():
        arrays[f"in_{name}_dram"] = a
        args.append(nc.dram_tensor(f"in_{name}_dram", a.shape, mybir.dt.from_np(a.dtype), kind="ExternalInput").ap())
    args.append(nc.dram_tensor("out_0_dram", (1, S, D), F32, kind="ExternalOutput").ap())
    hymba_layer(nc, *args)
    r = run_bass_kernel_spmd(nc, [arrays], core_ids=[0])
    return r.results[0]["out_0_dram"]
```

```python
import math
from contextlib import ExitStack

import numpy as np

import concourse.bass as bass
from concourse import mybir

F32 = mybir.dt.float32
F32R = mybir.dt.float32r
I32 = mybir.dt.int32
U32 = mybir.dt.uint32
ALU = mybir.AluOpType
ACT = mybir.ActivationFunctionType
AX_X = mybir.AxisListType.X

P = 128
D = 1024
KT = D // P
S = 512
NT = S // P
MEM = 256
DH = 64
HEADS = 4
DIL = ((128, 1), (512, 4), (2048, 16))
E = 32
TOPK = 4
FF = 1024
LIMIT = 7.0
ALPHA = 1.702
EPS = 1e-5
LAM_INIT = 0.8 - 0.6 * math.exp(-0.3 * 0)
SCALE = DH ** -0.5
NEG = -1e30

UC = 512
HALF = KT // 2 * UC
PHASE_A_UNITS = 8
MAX_BLOCKS = 48
MAX_LOOPS = 46
ROWS = S + P

C_IDENT, C_TRI, C_ONES, C_IOTA = 0, P, 2 * P, 3 * P
C_TOK = 4 * P
C_IDLE = C_TOK + NT
C_ROWMOD = C_IDLE + 1
N_CONST = C_ROWMOD + 1


def position_tables():
    p = np.arange(P)[:, None]
    dist = p - (np.arange(S)[None, :] - (S - P))
    slopes = [2.0 ** (-8.0 * (i + 1) / 8) for i in range(8)]
    out = np.full((8, P, S), NEG, np.float32)
    for h in range(HEADS):
        out[h] = np.where(dist >= 0, -slopes[2 * h] * dist / SCALE, NEG)
        count = sum(((dist % r == 0) & (dist <= w)).astype(int) for w, r in DIL) * (dist >= 0)
        term = (-slopes[2 * h + 1] * dist + np.log(np.maximum(count, 1))) / SCALE
        out[HEADS + h] = np.where(count > 0, term, NEG)
    return out.astype(np.float32)


def constants():
    c = np.zeros((P, N_CONST), np.float32)
    p = np.arange(P)
    c[:, C_IDENT:C_IDENT + P] = np.eye(P)
    c[:, C_TRI:C_TRI + P] = p[:, None] < p[None, :]
    c[:, C_ONES:C_ONES + P] = 1.0
    c[:, C_IOTA:C_IOTA + P] = p[None, :]
    for t in range(NT):
        c[:, C_TOK + t] = t * P + p + 1
    c[:, C_IDLE] = S + p + 1
    c[:, C_ROWMOD] = np.where(p < 2 * E, p % E, -1)
    return c


def attention_tasks():
    tasks = [("diff", h, qb) for qb in range(NT) for h in range(HEADS)]
    late = []
    for qb in range(NT):
        heads = [(kind, h, qb) for kind in ("dil", "mem") for h in range(HEADS)]
        if qb == 0:
            tasks += heads[:2] + [("mix", 0, t) for t in range(NT)] + heads[2:]
        else:
            tasks += heads[:1] + late + heads[1:]
        late = [("mix", 1, qb)]
    return tasks + [None] + late


def hymba_layer(nc, x, mem, attn_norm_g, mem_norm_g, w_in, diff_lambda_qk, diff_subln_g, w_mem_kv,
                w_out, ffn_norm_g, w_router, b_router, w_gate_up, b_gate_up, w_down, b_down,
                final_norm_g, const, postab, out):
    x_rows = x.rearrange("b (t p) d -> p (b t) d", p=P)
    mem_rows = mem.rearrange("b (t p) d -> p (b t) d", p=P)
    out_rows = out.rearrange("b (t p) d -> p (b t) d", p=P)
    h_dram = nc.dram_tensor("normed_rows", (S, D), F32).ap()
    sum_dram = nc.dram_tensor("sum_rows", (ROWS, D), F32).ap()

    def weight_columns(w, c):
        return w.rearrange("(k p) n -> p k n", p=P)[:, :, c * UC:(c + 1) * UC]

    phase_a = [weight_columns(w_mem_kv[0], 0)] + [weight_columns(w_in[0], c) for c in range(5)] \
        + [weight_columns(w_out[0], c) for c in range(2)]
    gu_dram = w_gate_up[0].rearrange("e (k p) n -> e p k n", p=P)
    dn_dram = w_down[0].rearrange("e (k p) n -> e p k n", p=P)

    with ExitStack() as ctx:
        def sb(name, shape, dt):
            return ctx.enter_context(nc.sbuf_tensor(name, shape, dt))

        def sem(name):
            return ctx.enter_context(nc.semaphore(name))

        raw = sb("raw", [P, 6, HALF], F32)
        w_hi = sb("w_hi", [P, 4, HALF], F32R)
        w_lo = sb("w_lo", [P, 4, HALF], F32R)
        R = sb("turned", [P, 2 * KT * S], F32R)
        F = sb("arena", [P, 15360], F32)
        cst = sb("cst", [P, N_CONST], F32)
        gains = sb("gains", [P, 3 * KT + 1], F32)
        stat = sb("stat", [P, 8, 8], F32)
        nrm = sb("nrm", [P, 4, 16], F32)
        lamw = sb("lamw", [P, 8], F32)
        psum = [ctx.enter_context(nc.psum_tensor(f"bank{i}", [P, 512], F32)) for i in range(8)]

        ident = cst[:, C_IDENT:C_IDENT + P]
        tri = cst[:, C_TRI:C_TRI + P]
        ones = cst[:, C_ONES:C_ONES + P]
        iota = cst[:, C_IOTA:C_IOTA + P]
        g_attn, g_mem, g_ffn = (gains[:, i * KT:(i + 1) * KT] for i in range(3))
        g_mix = gains[:, 3 * KT:3 * KT + 1]

        act_hi = R[:, 0:KT * S].rearrange("p (k s) -> p k s", k=KT)
        act_lo = R[:, KT * S:].rearrange("p (k s) -> p k s", k=KT)

        xr = F[:, 0:4096].rearrange("p (t d) -> p t d", t=NT)
        mr = F[:, 4096:6144].rearrange("p (t d) -> p t d", t=2)
        junk = F[:, 13312:14336]
        lam_in = F[:, 14336:14592].rearrange("p (a d) -> p a d", a=4)
        gain_rows = F[0:3 * KT + 1, 14592:14592 + P]
        qk = F[:, 0:7168].rearrange("p (i s) -> p i s", i=14)
        dil_v = F[:, 7168:8192].rearrange("p (t n) -> p t n", t=NT)
        mem_v = F[:, 8192:8704].rearrange("p (t n) -> p t n", t=2)
        mem_k = F[:, 8704:9216].rearrange("p (t n) -> p t n", t=2)
        pos = F[:, 9216:13312].rearrange("p (h u) -> p h u", h=8)
        probs = F[:, 13312:15360].rearrange("p (i j s) -> p i j s", i=2, j=2)
        diff_v = raw[:, 4, :].rearrange("p (t n) -> p t n", t=NT)
        pt = raw[:, 5, 0:1024].rearrange("p (i s) -> p i s", i=2)
        mix = raw[:, 5, 1024:2048].rearrange("p (i n) -> p i n", i=2)

        xn = F[:, 4096:8192].rearrange("p (t d) -> p t d", t=NT)
        hT = F[:, 8192:10240].rearrange("p (i k s) -> p i k s", i=2, k=KT)
        w_rt = F[:, 10240:10496].rearrange("p (k e) -> p k e", k=KT)
        at = [10496]

        def small(n):
            at[0] += n
            assert at[0] <= 12288
            return F[:, at[0] - n:at[0]]

        lg = small(NT * E).rearrange("p (t e) -> p t e", t=NT)
        top = small(NT * 8).rearrange("p (t k) -> p t k", t=NT)
        top_i = small(NT * 8).bitcast(U32).rearrange("p (t k) -> p t k", t=NT)
        top_f = small(NT * 8).rearrange("p (t k) -> p t k", t=NT)
        ntop = small(NT)
        gate_e = small(NT * TOPK).rearrange("p (t k) -> p t k", t=NT)
        gate_s = small(NT)
        picked = small(NT * TOPK * E).rearrange("p (t k e) -> p t k e", t=NT, k=TOPK)
        picked_slot = F[:, 9728:10240].rearrange("p (t k e) -> p t k e", t=NT, k=TOPK)
        chosen = small(NT * E).rearrange("p (t e) -> p t e", t=NT)
        n_blk = small(E)
        cum = small(4 * E).rearrange("p (i e) -> p i e", i=2)
        b_start = small(E)
        slots = small(NT * E).rearrange("p (t e) -> p t e", t=NT)
        slot_f = small(NT * TOPK)
        slot_i = small(NT * TOPK).bitcast(I32)
        loc_i = small(NT * TOPK).bitcast(I32)
        blk_i = small(NT * TOPK).bitcast(I32)
        loc_f = small(NT * TOPK)
        blk_f = small(NT * TOPK)
        br_row = small(E)[0:1, :]
        lane_hot = F[:, 12288:14336].rearrange("p (i s) -> p i s", i=NT * TOPK)
        blk_hot = F[:, 8192:10496].rearrange("p (i j b) -> p i j b", i=NT * TOPK, j=3)
        e_cmp = F[:, 8192:9728].rearrange("p (b e) -> p b e", b=MAX_BLOCKS)
        tabs = F[:, 14336:14336 + 8 * MAX_BLOCKS].rearrange("p (i b) -> p i b", i=8)
        tok_f, gate_t, exp_f, idle_f = (tabs[:, i, :] for i in range(4))
        sum_row_i = tabs[:, 4, :].bitcast(I32)
        tok_i = tabs[:, 5, :].bitcast(I32)
        exp_i = tabs[:, 6, :].bitcast(I32)
        loops_i = tabs[:, 7, 0:1].bitcast(I32)
        idx_gather = F[:, 15000:15001].bitcast(I32)
        idx_scatter = F[:, 15001:15002].bitcast(I32)

        bias_in = F[0:2 * E, 0:3 * FF]
        h_row = F[:, 4096:5120]
        act = F[:, 5120:6144]
        y_row = F[:, 6144:7168]
        gate_c, up_c, prod_c, sig_c = (F[:, 7168 + 512 * i:7680 + 512 * i].rearrange("p (i n) -> p i n", i=2)
                                       for i in range(4))
        g_final = F[:, 9728:10752]
        hx, lx = (R[:, i * D:(i + 1) * D].rearrange("p (k s) -> p k s", k=KT) for i in (0, 1))
        ha, la = (R[:, i * D:(i + 1) * D].rearrange("p (k s) -> p k s", k=KT) for i in (2, 3))
        bias = R[:, 4 * D:7 * D]
        pick = R[:, 7 * D:7 * D + P]
        pick_y = R[:, 7 * D + P:7 * D + 2 * P]

        gains_turned, gains_ready = sem("gains_turned"), sem("gains_ready")
        const_in, gains_in, mem_in, x_in, pos_in, lam_in_s = (
            sem(n) for n in ("const_in", "gains_in", "mem_in", "x_in", "pos_in", "lam_in_s"))
        raw_in = [sem(f"raw_in{i}") for i in range(6)]
        hi_ready, lo_ready, half_used = sem("hi_ready"), sem("lo_ready"), sem("half_used")
        dve_seq = sem("dve_seq")
        squares = sem("squares")
        normed = sem("normed")
        turn_in, turn_hi, turn_lo = sem("turn_in"), sem("turn_hi"), sem("turn_lo")
        proj_in, proj_out = sem("proj_in"), sem("proj_out")
        lam_dots, lam_exp, lam_ready = sem("lam_dots"), sem("lam_exp"), sem("lam_ready")
        sc_ready, max_done, exp_done, prob_ready = (
            sem(n) for n in ("sc_ready", "max_done", "exp_done", "prob_ready"))
        pt_in, pt_out, mix_lo, pv_done, out_done = (
            sem(n) for n in ("pt_in", "pt_out", "mix_lo", "pv_done", "out_done"))
        x_again, wo_done, x1_ready = sem("x_again"), sem("wo_done"), sem("x1_ready")
        rows_out = sem("rows_out")
        router_in, router_g = sem("router_in"), sem("router_g")
        ht_in, ht_out, lg_in, lg_out = sem("ht_in"), sem("ht_out"), sem("lg_in"), sem("lg_out")
        top_ready, gates_e = sem("top_ready"), sem("gates_e")
        gather_go, scatter_go = sem("gather_go"), sem("scatter_go")
        chosen_ready, rank_in, hot_ready, tab_in, tab_ready = (
            sem(n) for n in ("chosen_ready", "rank_in", "hot_ready", "tab_in", "tab_ready"))
        bias_in_s, bias_ready = sem("bias_in_s"), sem("bias_ready")
        idx_ready, h_in, y_sent, x1_sent = (sem(n) for n in ("idx_ready", "h_in", "y_sent", "x1_sent"))
        xtp_done, xhi_ready, xlo_ready = sem("xtp_done"), sem("xhi_ready"), sem("xlo_ready")
        atp_done, ahi_ready, alo_ready = sem("atp_done"), sem("ahi_ready"), sem("alo_ready")
        pick_ready, pick_y_ready, ybias_done = sem("pick_ready"), sem("pick_y_ready"), sem("ybias_done")
        gu_done, gu_free, gate_ready, sig_ready, prod_ready, act_ready = (
            sem(n) for n in ("gu_done", "gu_free", "gate_ready", "sig_ready", "prod_ready", "act_ready"))
        y_free = sem("y_free")
        gf_in, fin_in, fin_out = sem("gf_in"), [sem(f"fin_in{t}") for t in range(NT)], sem("fin_out")
        out_sent = sem("out_sent")

        tasks = attention_tasks()
        real = {t: i for i, t in enumerate(t for t in tasks if t and t[0] != "mix")}
        turned = {t: i for i, t in enumerate(t for t in tasks if t)}
        by_turn = list(turned)
        NR, NTURN = len(real), len(turned)
        LAG_T, LAG_V = 2, 3
        STEPS = len(tasks) + LAG_V

        def out_bank(r):
            return 1 if r > HEADS * NT and r % 2 else 6

        def task(i):
            return tasks[i] if 0 <= i < len(tasks) else None

        def is_real(t):
            return t is not None and t[0] != "mix"

        def n_keys(t):
            return MEM if t[0] == "mem" else P * (t[2] + 1)

        def turned_index(r):
            return turned[list(real)[r]]

        TILES = [(0, MEM, True, 0, 0), (0, MEM, True, P, 0), (0, MEM, False, MEM, 0), (0, MEM, False, MEM, P)]
        for u in (1, 2, 3, 4):
            TILES += [(u, 512, False, 0, t * P) if u == 3 else (u, S, True, t * P, 0) for t in range(NT)]
        TILES += [(5, 256, False, 0, t * P) for t in range(NT)] + [(5, S, True, 256 + j * P, 0) for j in range(2)]
        N_IN = len(TILES)
        N_DENSE = 16
        TILES += [(u, 512, False, 0, t * P) for t in range(NT) for u in (6, 7)]
        TILES = [t + (all(other[0] != t[0] for other in TILES[n + 1:]),) for n, t in enumerate(TILES)]

        def proj_bank(n):
            return n % 4 if n < N_DENSE else 0 if n == len(TILES) - 1 else 7

        FILL, at_step = {}, 0
        for n in range(N_DENSE, len(TILES)):
            if n >= N_IN:
                at_step = max(at_step, tasks.index(("mix", 1, (n - N_IN) // 2)) + LAG_V + 1)
            for part in ((None,) if TILES[n][1] == 256 else (0, 1)):
                FILL[at_step] = (n, part)
                at_step += 1
        DONE = {i + 1: n for i, (n, part) in FILL.items() if part != 0}
        SPLIT = {1: 10, 3: 11, 9: 12, 11: 13, 17: 14, 19: 15}
        ALL_STEPS = max(STEPS, max(DONE) + 1)

        def wait_tile(eng, n):
            if TILES[n][5]:
                eng.wait_ge(half_used, 2 * TILES[n][0] + 2)
            else:
                eng.wait_ge(proj_in, sum(not t[5] for t in TILES[:n + 1]))

        def raw_slot(m, h):
            return (2 * m + h) % 6

        def raw_value(m, h):
            return 16 * ((4 if raw_slot(m, h) < 4 else 0) + (2 * m + h) // 6 + 1)

        block = ctx.enter_context(nc.Block())

        @block.sync
        def _(sp):
            sp.dma_start(mr, mem_rows).then_inc(mem_in, 16)
            sp.dma_start(cst[:, :], const).then_inc(const_in, 16)
            for i, g in enumerate((attn_norm_g, mem_norm_g, ffn_norm_g)):
                sp.dma_start(gain_rows[i * KT:(i + 1) * KT, :], g.rearrange("o (k p) -> (o k) p", p=P)).then_inc(gains_in, 16)
            sp.dma_start(gain_rows[3 * KT:, :], diff_subln_g).then_inc(gains_in, 16)
            def first_phase(half):
                u, k0 = half // 2, half % 2 * (KT // 2)
                sp.dma_start(raw[:, half % 4, :].rearrange("p (k n) -> p k n", k=KT // 2),
                             phase_a[u][:, k0:k0 + KT // 2, :]).then_inc(raw_in[half % 4], 16)

            first_phase(0)
            first_phase(1)
            sp.dma_start(xr, x_rows).then_inc(x_in, 16)
            for half in range(2, 2 * PHASE_A_UNITS):
                if half >= 4:
                    sp.wait_ge(lo_ready, half - 3)
                first_phase(half)
                if half == 3:
                    sp.dma_start(pos, postab.rearrange("h p u -> p h u")).then_inc(pos_in, 16)
            sp.wait_ge(pt_in, turned[("mix", 0, NT - 1)] + 1)
            sp.dma_start(xr, x_rows).then_inc(x_again, 16)

            def gate_up(e, c, m, b=None):
                for h in range(2):
                    if b is not None or 2 * m + h >= 6:
                        sp.wait_ge(lo_ready, 11 + 2 * m + h if b is None else b * 12 + (11 + 2 * m + h))
                    sp.dma_start(raw[:, raw_slot(m, h), :].rearrange("p (k n) -> p k n", k=KT // 2),
                                 gu_dram[bass.ds(e, 1), :, h * (KT // 2):(h + 1) * (KT // 2), c * UC:(c + 1) * UC]
                                 .rearrange("e p k n -> p (e k) n")).then_inc(raw_in[raw_slot(m, h)], 16)

            def down(e, c, m, b=None):
                for h in range(2):
                    sp.wait_ge(lo_ready, 11 + 2 * m + h if b is None else b * 12 + (11 + 2 * m + h))
                    k0 = c * (KT // 2) + h * (KT // 4)
                    sp.dma_start(raw[:, raw_slot(m, h), :].rearrange("p (k n) -> p k n", k=KT // 4),
                                 dn_dram[bass.ds(e, 1), :, k0:k0 + KT // 4, :]
                                 .rearrange("e p k n -> p (e k) n")).then_inc(raw_in[raw_slot(m, h)], 16)

            sp.wait_ge(lo_ready, 14)
            gate_up(0, 0, 0)
            sp.wait_ge(lo_ready, 16)
            gate_up(0, 1, 1)
            sp.wait_ge(mix_lo, 2 * NT)
            sp.wait_ge(pv_done, NR)
            gate_up(0, 2, 2)
            sp.wait_ge(wo_done, 2 * NT)
            sp.dma_start(sum_dram[0:S, :].rearrange("(t p) d -> p t d", p=P), xr).then_inc(x1_sent, 16)
            for t in range(NT):
                sp.wait_ge(normed, 6 + t + 1)
                sp.dma_start(h_dram[t * P:(t + 1) * P, :], xn[:, t, :]).then_inc(rows_out, 16)
            gate_up(0, 3, 3)
            sp.wait_ge(tab_ready, 1)
            loops = sp.value_load(loops_i[0:1, :], min_val=E - 1, max_val=MAX_LOOPS)
            gate_up(sp.value_load(exp_i[0:1, 1:2], min_val=0, max_val=E - 1), 0, 4)
            down(0, 0, 5)
            with sp.Fori(1, loops) as b:
                before, e, after = (sp.value_load(exp_i[0:1, bass.ds(b + i, 1)], min_val=0, max_val=E - 1)
                                    for i in (-1, 0, 1))
                gate_up(e, 1, 0, b)
                gate_up(e, 2, 1, b)
                gate_up(e, 3, 2, b)
                down(before, 1, 3, b)
                gate_up(after, 0, 4, b)
                down(e, 0, 5, b)
            before = sp.value_load(exp_i[0:1, bass.ds(loops - 1, 1)], min_val=0, max_val=E - 1)
            e = sp.value_load(exp_i[0:1, bass.ds(loops, 1)], min_val=0, max_val=E - 1)
            gate_up(e, 1, 0, loops)
            gate_up(e, 2, 1, loops)
            gate_up(e, 3, 2, loops)
            down(before, 1, 3, loops)
            down(e, 0, 4, loops)
            down(e, 1, 5, loops)
            sp.wait_ge(y_sent, loops * 16 + 32)
            for t in range(NT):
                sp.dma_start(xr[:, t, :], sum_dram[t * P:(t + 1) * P, :]).then_inc(fin_in[t], 16)
            for t in range(NT):
                sp.wait_ge(fin_out, t + 1)
                sp.dma_start(out_rows[:, t, :], xr[:, t, :]).then_inc(out_sent, 16)
            sp.wait_ge(rows_out, 16 * NT)
            sp.wait_ge(out_sent, 16 * NT)

        @block.gpsimd
        def _(pool):
            pool.dma_start(lam_in, diff_lambda_qk.to_broadcast([P, 4, DH])).then_inc(lam_in_s, 16)
            pool.wait_ge(exp_done, NR)
            pool.dma_start(w_rt, w_router[0].rearrange("(k p) e -> p k e", p=P)).then_inc(router_in, 16)
            pool.dma_start(br_row, b_router).then_inc(router_in, 16)
            pool.wait_ge(normed, 6 + NT)
            pool.wait_ge(x1_sent, 16)
            pool.dma_start(sum_dram[S:ROWS, :], xn[:, 0, :]).then_inc(y_sent, 16)
            for i in range(2):
                pool.dma_start(F[i * E:(i + 1) * E, 0:2 * FF], b_gate_up[0]).then_inc(bias_in_s, 16)
                pool.dma_start(F[i * E:(i + 1) * E, 2 * FF:3 * FF], b_down[0]).then_inc(bias_in_s, 16)
            pool.wait_ge(tab_ready, 1)
            pool.wait_ge(rows_out, 16 * NT)
            pool.dma_start(g_final, final_norm_g.unsqueeze(0).to_broadcast([P, D])).then_inc(gf_in, 16)
            loops = pool.value_load(loops_i[0:1, :], min_val=E - 1, max_val=MAX_LOOPS)

            def gather(column, n):
                n = n if isinstance(n, int) else pool.snap(n)
                pool.tensor_copy(idx_gather, tok_i[:, column]).then_inc(idx_ready, 1)
                pool.wait_ge(idx_ready, n)
                pool.sem_inc(gather_go, 1)
                pool.indirect_dma_start(h_row, None, h_dram,
                                        bass.IndirectOffsetOnAxis(idx_gather, 0)).then_inc(h_in, 16)

            gather(slice(0, 1), 1)
            for b in (0, 1):
                pool.wait_ge(xtp_done, b + 1)
                gather(slice(b + 1, b + 2), b + 2)

            def scatter(b, n_idx):
                copied, rows, sent = pool.snap(n_idx), pool.snap(b + 2), pool.snap(b * 16 + 16)
                pool.wait_ge(y_sent, sent)
                pool.tensor_copy(idx_scatter, sum_row_i[:, bass.ds(b, 1)]).then_inc(idx_ready, 1)
                pool.wait_ge(idx_ready, copied)
                pool.wait_ge(y_free, rows)
                pool.sem_inc(scatter_go, 1)
                pool.indirect_dma_start(sum_dram, bass.IndirectOffsetOnAxis(idx_scatter, 0),
                                        y_row, None, compute_op=ALU.add).then_inc(y_sent, 16)

            with pool.Fori(1, loops) as b:
                pool.wait_ge(xtp_done, b + 2)
                gather(bass.ds(b + 2, 1), b * 2 + 2)
                scatter(b - 1, b * 2 + 3)
            scatter(loops - 1, loops * 2 + 2)
            scatter(loops, loops * 2 + 3)
            pool.wait_ge(y_sent, loops * 16 + 32)
            pool.wait_ge(h_in, loops * 16 + 32)

        @block.scalar
        def _(a):
            def hi(half, slot, raw_ap, raw_sem, value):
                a.wait_ge(raw_sem, value)
                if not isinstance(half, int) or half >= 4:
                    a.wait_ge(half_used, half - 3)
                a.activation(w_hi[:, slot, :], raw_ap, ACT.Copy).then_inc(hi_ready, 1)

            def hi_a(half):
                hi(half, half % 4, raw[:, half % 4, :], raw_in[half % 4], 16 * (half // 4 + 1))

            def hi_m(m, h, b=None):
                half = 16 + 2 * m + h
                value = raw_value(m, h)
                hi(half if b is None else b * 12 + half, half % 4, raw[:, raw_slot(m, h), :],
                   raw_in[raw_slot(m, h)], value if b is None else b * 32 + value)

            def mean_square(src, col):
                a.activation(junk, src, ACT.Square, scale=1.0 / math.sqrt(D),
                             accum_out=nrm[:, 0, col:col + 1]).then_inc(squares, 1)

            a.wait_ge(mem_in, 16)
            for t in range(2):
                if t:
                    a.wait_ge(squares, t)
                mean_square(mr[:, t, :], t)
            hi_a(0)
            hi_a(1)
            a.wait_ge(gains_ready, 1)
            for k in range(KT):
                a.wait_ge(turn_in, k + 1)
                a.activation(act_hi[:, k, 0:MEM], psum[k][:, 0:MEM], ACT.Copy,
                             scale=g_mem[:, k:k + 1]).then_inc(turn_hi, 1)
            a.wait_ge(x_in, 16)
            a.wait_ge(normed, 2)
            for t in range(NT):
                a.wait_ge(squares, 2 + t)
                mean_square(xr[:, t, :], t)
            a.wait_ge(lam_dots, 1)
            a.activation(lamw[:, 2:4], lamw[:, 0:2], ACT.Exp).then_inc(lam_exp, 1)
            hi_a(2)
            hi_a(3)

            def proj_evac(n, dst, width):
                wait_tile(a, n)
                a.activation(dst, psum[proj_bank(n)][:, 0:width], ACT.Copy).then_inc(proj_out, 1)

            for j in range(2):
                proj_evac(j, mem_k[:, j, :], MEM)
            for t in range(2):
                proj_evac(2 + t, mem_v[:, t, :], MEM)
            for k in range(KT):
                a.wait_ge(turn_in, KT + k + 1)
                a.activation(act_hi[:, k, :], psum[k][:, :], ACT.Copy,
                             scale=g_attn[:, k:k + 1]).then_inc(turn_hi, 1)
            n = 4
            dsts = [(qk[:, i, :], S) for i in range(8)] + [(diff_v[:, t, :], 512) for t in range(NT)]
            dsts += [(qk[:, 8 + i, :], S) for i in range(4)]
            dsts += [(dil_v[:, t, :], 256) for t in range(NT)] + [(qk[:, 12 + i, :], S) for i in range(2)]
            for n in range(4, N_DENSE):
                if n % 4 == 0:
                    hi_a(n // 2 + 2)
                    hi_a(n // 2 + 3)
                proj_evac(n, *dsts[n - 4])

            for i in range(STEPS):
                if DONE.get(i, N_IN) < N_IN:
                    proj_evac(DONE[i], *dsts[DONE[i] - 4])
                if i in SPLIT:
                    hi_a(SPLIT[i])
                t = task(i - LAG_T)
                if t is not None:
                    ti = turned[t]
                    a.wait_ge(pt_in, ti + 1)
                    if t[0] == "mix":
                        src = psum[4 + ti % 2][:, :].rearrange("p (k s) -> p k s", k=4)
                        dst = act_hi[:, 4 * t[1]:4 * t[1] + 4, t[2] * P:(t[2] + 1) * P]
                        a.activation(dst, src, ACT.Copy,
                                     scale=g_mix if t[1] == 0 else 1.0).then_inc(pt_out, 1)
                    else:
                        r = real[t]
                        if r >= 2:
                            a.wait_ge(pv_done, r - 1)
                        n = n_keys(t)
                        a.activation(pt[:, r % 2, 0:n], psum[4 + ti % 2][:, 0:n], ACT.Copy).then_inc(pt_out, 1)
                t = task(i)
                if is_real(t):
                    r = real[t]
                    st = stat[:, r % 8, :]
                    n = n_keys(t)
                    a.wait_ge(max_done, r + 1)
                    if t[0] == "mem":
                        if r >= 2:
                            a.wait_ge(pt_in, turned_index(r - 2) + 1)
                        a.activation(probs[:, r % 2, 0, 0:n], psum[2 * (r % 2)][:, 0:n], ACT.Exp,
                                     bias=st[:, 2:3], scale=SCALE, accum_out=st[:, 4:5]).then_inc(exp_done, 1)
                    else:
                        branches = 2 if t[0] == "diff" else 1
                        for j in range(branches):
                            ins = a.activation(probs[:, r % 2, j, 0:n], probs[:, r % 2, j, 0:n], ACT.Exp,
                                               bias=st[:, 2 + j:3 + j], accum_out=st[:, 4 + j:5 + j])
                        ins.then_inc(exp_done, 1)

            for t in range(NT):
                a.wait_ge(wo_done, 2 * t + 2)
                a.wait_ge(squares, 6 + t)
                mean_square(xr[:, t, :], t)
            for t in range(NT):
                for q in range(2):
                    i = 2 * t + q
                    a.wait_ge(ht_in, i + 1)
                    if t >= 2:
                        a.wait_ge(lg_in, t - 1)
                    a.activation(hT[:, t % 2, 4 * q:4 * q + 4, :],
                                 psum[i % 4][:, :].rearrange("p (k s) -> p k s", k=4), ACT.Copy).then_inc(ht_out, 1)
                hi_m(t // 2, t % 2)
            a.wait_ge(top_ready, 1)
            for t in range(NT):
                a.activation(gate_e[:, t, :], top[:, t, 0:TOPK], ACT.Exp, bias=ntop[:, t:t + 1],
                             accum_out=gate_s[:, t:t + 1]).then_inc(gates_e, 1)

            def turn_x(q, n):
                a.wait_ge(xtp_done, n)
                bank = psum[6 + q][:, :].rearrange("p (k s) -> p k s", k=4)
                for k in range(4):
                    ins = a.activation(hx[:, 4 * q + k, :], bank[:, k, :], ACT.Copy,
                                       scale=g_ffn[:, 4 * q + k:4 * q + k + 1])
                ins.then_inc(xhi_ready, 1)

            def turn_act(q, n):
                a.wait_ge(atp_done, n)
                a.activation(ha[:, 4 * q:4 * q + 4, :],
                             psum[6 + q][:, :].rearrange("p (k s) -> p k s", k=4), ACT.Copy).then_inc(ahi_ready, 1)

            def sigmoid(c, n):
                a.wait_ge(gate_ready, n)
                a.activation(sig_c[:, c % 2, :], gate_c[:, c % 2, :], ACT.Sigmoid,
                             scale=ALPHA).then_inc(sig_ready, 1)

            def y_out(used, column, sent):
                a.wait_ge(half_used, used)
                a.wait_ge(y_sent, sent)
                for c in range(2):
                    ins = a.activation(y_row[:, c * 512:(c + 1) * 512], psum[4 + c][:, :], ACT.Copy,
                                       scale=gate_t[:, column])
                ins.then_inc(y_free, 1)

            a.wait_ge(tab_ready, 1)
            a.sem_inc(y_free, 1)
            loops = a.value_load(loops_i[0:1, :], min_val=E - 1, max_val=MAX_LOOPS)
            turn_x(0, 1)
            turn_x(1, 1)
            hi_m(2, 0)
            hi_m(2, 1)
            hi_m(3, 0)
            sigmoid(0, 1)
            hi_m(3, 1)
            hi_m(4, 0)
            sigmoid(1, 2)
            hi_m(4, 1)
            sigmoid(2, 3)
            a.wait_ge(half_used, 16 + 2 * 3 + 1)
            turn_x(0, 2)
            a.wait_ge(half_used, 16 + 2 * 3 + 2)
            turn_x(1, 2)
            sigmoid(3, 4)
            hi_m(5, 0)
            turn_act(0, 1)
            hi_m(5, 1)
            with a.Fori(1, loops) as b:
                hi_m(0, 0, b)
                turn_act(1, b * 2)
                sigmoid(0, b * 4 + 1)
                hi_m(0, 1, b)
                hi_m(1, 0, b)
                hi_m(1, 1, b)
                hi_m(2, 0, b)
                sigmoid(1, b * 4 + 2)
                hi_m(2, 1, b)
                hi_m(3, 0, b)
                sigmoid(2, b * 4 + 3)
                a.wait_ge(half_used, b * 12 + (16 + 2 * 2 + 1))
                turn_x(0, b + 2)
                hi_m(3, 1, b)
                a.wait_ge(half_used, b * 12 + (16 + 2 * 2 + 2))
                turn_x(1, b + 2)
                hi_m(4, 0, b)
                hi_m(4, 1, b)
                sigmoid(3, b * 4 + 4)
                y_out(b * 12 + (16 + 2 * 3 + 2), bass.ds(b - 1, 1), b * 16)
                hi_m(5, 0, b)
                turn_act(0, b * 2 + 1)
                hi_m(5, 1, b)
            b = loops
            hi_m(0, 0, b)
            turn_act(1, b * 2)
            sigmoid(0, b * 4 + 1)
            hi_m(0, 1, b)
            hi_m(1, 0, b)
            hi_m(1, 1, b)
            hi_m(2, 0, b)
            sigmoid(1, b * 4 + 2)
            hi_m(2, 1, b)
            hi_m(3, 0, b)
            sigmoid(2, b * 4 + 3)
            hi_m(3, 1, b)
            hi_m(4, 0, b)
            sigmoid(3, b * 4 + 4)
            y_out(b * 12 + (16 + 2 * 3 + 2), bass.ds(b - 1, 1), b * 16)
            turn_act(0, b * 2 + 1)
            hi_m(4, 1, b)
            hi_m(5, 0, b)
            turn_act(1, b * 2 + 2)
            hi_m(5, 1, b)
            y_out(b * 12 + (16 + 2 * 5 + 2), bass.ds(b, 1), b * 16 + 16)
            for t in range(NT):
                a.wait_ge(fin_in[t], 16)
                a.wait_ge(squares, 10 + t)
                mean_square(xr[:, t, :], t)

        @block.vector
        def _(v):
            seq = [0]

            def link(ins):
                seq[0] += 1
                ins.then_inc(dve_seq, 1)
                v.wait_ge(dve_seq, seq[0])

            def rsqrt(n):
                ms, y, t1, t2 = (nrm[:, i, 0:n] for i in range(4))
                link(v.tensor_scalar(ms, ms, EPS, None, ALU.add))
                link(v.tensor_scalar(t1.bitcast(I32), ms.bitcast(I32), 1, None, ALU.arith_shift_right))
                link(v.tensor_scalar(y.bitcast(I32), t1.bitcast(I32), -1, 0x5F3759DF, ALU.mult, ALU.add))
                for _ in range(3):
                    link(v.scalar_tensor_tensor(out=t1, in0=y, scalar=-0.5, in1=y, op0=ALU.mult, op1=ALU.mult))
                    link(v.tensor_tensor(t2, t1, ms, ALU.mult))
                    link(v.scalar_tensor_tensor(out=y, in0=t2, scalar=1.5, in1=y, op0=ALU.add, op1=ALU.mult))

            def lo(half, slot, raw_ap):
                v.wait_ge(hi_ready, half + 1)
                v.tensor_tensor(w_lo[:, slot, :], raw_ap, w_hi[:, slot, :].bitcast(F32),
                                ALU.subtract).then_inc(lo_ready, 1)

            def lo_a(half):
                lo(half, half % 4, raw[:, half % 4, :])

            def lo_m(m, h, b=None):
                half = 16 + 2 * m + h
                lo(half if b is None else b * 12 + half, half % 4, raw[:, raw_slot(m, h), :])

            v.wait_ge(gains_turned, 1)
            link(v.tensor_copy(gains[:, :], psum[0][:, 0:3 * KT + 1]))
            v.tensor_scalar(g_mix, g_mix, 1.0 - LAM_INIT, None, ALU.mult).then_inc(gains_ready, 1)
            v.wait_ge(gains_ready, 1)
            v.wait_ge(squares, 2)
            rsqrt(2)
            for t in range(2):
                v.tensor_scalar(mr[:, t, :], mr[:, t, :], nrm[:, 1, t:t + 1], None, ALU.mult).then_inc(normed, 1)
            lo_a(0)
            lo_a(1)
            for k in range(KT):
                v.wait_ge(turn_hi, k + 1)
                v.scalar_tensor_tensor(out=act_lo[:, k, 0:MEM], in0=psum[k][:, 0:MEM], scalar=g_mem[:, k:k + 1],
                                       in1=act_hi[:, k, 0:MEM].bitcast(F32), op0=ALU.mult,
                                       op1=ALU.subtract).then_inc(turn_lo, 1)
            v.wait_ge(lam_in_s, 16)
            for j in range(2):
                link(v.tensor_tensor_reduce(lam_in[:, 2 * j, :], lam_in[:, 2 * j, :], lam_in[:, 2 * j + 1, :],
                                            1.0, 0.0, ALU.mult, ALU.add, lamw[:, j:j + 1]))
            v.tensor_copy(lamw[:, 6:8], lamw[:, 0:2]).then_inc(lam_dots, 1)
            v.wait_ge(squares, 2 + NT)
            rsqrt(NT)
            for t in range(NT):
                v.tensor_scalar(xr[:, t, :], xr[:, t, :], nrm[:, 1, t:t + 1], None, ALU.mult).then_inc(normed, 1)
            lo_a(2)
            lo_a(3)
            v.wait_ge(lam_exp, 1)
            link(v.tensor_tensor(lamw[:, 4:5], lamw[:, 3:4], lamw[:, 2:3], ALU.subtract))
            link(v.tensor_scalar(lamw[:, 5:6], lamw[:, 4:5], LAM_INIT, None, ALU.subtract))
            for k in range(KT):
                v.wait_ge(turn_hi, KT + k + 1)
                v.scalar_tensor_tensor(out=act_lo[:, k, :], in0=psum[k][:, :], scalar=g_attn[:, k:k + 1],
                                       in1=act_hi[:, k, :].bitcast(F32), op0=ALU.mult,
                                       op1=ALU.subtract).then_inc(turn_lo, 1)
            for half in range(4, 10):
                lo_a(half)

            v.wait_ge(pos_in, 16)

            def soft(t):
                r = real[t]
                st = stat[:, r % 8, :]
                n = n_keys(t)
                v.wait_ge(sc_ready, r + 1)
                if t[0] == "mem":
                    link(v.tensor_reduce(st[:, 0:1], psum[2 * (r % 2)][:, 0:n], AX_X, ALU.max))
                    v.tensor_scalar(st[:, 2:3], st[:, 0:1], -SCALE, None, ALU.mult).then_inc(max_done, 1)
                    return
                if r >= 2:
                    v.wait_ge(pt_in, turned_index(r - 2) + 1)
                branches = 2 if t[0] == "diff" else 1
                table = t[1] if t[0] == "diff" else HEADS + t[1]
                for j in range(branches):
                    link(v.tensor_tensor_reduce(probs[:, r % 2, j, 0:n], psum[2 * (r % 2) + j][:, 0:n],
                                                pos[:, table, S - n:S], SCALE, NEG, ALU.add, ALU.max,
                                                st[:, j:j + 1]))
                v.tensor_scalar(st[:, 2:2 + branches], st[:, 0:branches], -1.0, None,
                                ALU.mult).then_inc(max_done, 1)

            def combine(t):
                r = real[t]
                st = stat[:, r % 8, :]
                n = n_keys(t)
                v.wait_ge(exp_done, r + 1)
                if t[0] != "diff":
                    v.reciprocal(st[:, 6:7], st[:, 4:5]).then_inc(prob_ready, 1)
                    return
                link(v.reciprocal(st[:, 6:8], st[:, 4:6]))
                link(v.tensor_scalar(st[:, 7:8], st[:, 7:8], lamw[:, 5:6], None, ALU.mult))
                p1, p2 = probs[:, r % 2, 0, 0:n], probs[:, r % 2, 1, 0:n]
                link(v.tensor_scalar(p1, p1, st[:, 6:7], None, ALU.mult))
                v.scalar_tensor_tensor(out=p1, in0=p2, scalar=st[:, 7:8], in1=p1, op0=ALU.mult,
                                       op1=ALU.add).then_inc(prob_ready, 1)

            mixes = [0]

            def finish(t):
                if t[0] == "mix":
                    ti = turned[t]
                    mixes[0] += 1
                    v.wait_ge(pt_out, ti + 1)
                    src = psum[4 + ti % 2][:, :].rearrange("p (k s) -> p k s", k=4)
                    part = (slice(None), slice(4 * t[1], 4 * t[1] + 4), slice(t[2] * P, (t[2] + 1) * P))
                    v.scalar_tensor_tensor(out=act_lo[part], in0=src, scalar=g_mix if t[1] == 0 else 1.0,
                                           in1=act_hi[part].bitcast(F32), op0=ALU.mult,
                                           op1=ALU.subtract).then_inc(mix_lo, 1)
                    return
                kind, h, qb = t
                r = real[t]
                o = psum[out_bank(r)]
                v.wait_ge(pv_done, r + 1)
                if kind != "diff":
                    if qb >= 2 and (kind, h) == ("dil", 0):
                        v.wait_ge(pt_in, turned[("mix", 1, qb - 2)] + 1)
                    at0 = 256 * (kind == "mem") + h * DH
                    v.tensor_scalar(mix[:, qb % 2, at0:at0 + DH], o[:, 0:DH], stat[:, r % 8, 6:7], None,
                                    ALU.mult).then_inc(out_done, 1)
                    return
                mine = qk[:, h, qb * P:(qb + 1) * P]
                link(v.tensor_copy(mine, o[:, 0:P]))
                ins = v.tensor_tensor_reduce(o[:, P:2 * P], mine, mine, 1.0 / P, 0.0, ALU.mult, ALU.add,
                                             nrm[:, 0, h * NT + qb:h * NT + qb + 1])
                if (h, qb) != (HEADS - 1, NT - 1):
                    ins.then_inc(out_done, 1)
                    return
                link(ins)
                rsqrt(HEADS * NT)
                rows = qk[:, 0:HEADS, :].rearrange("p h (q d) -> p (h q) d", q=NT)
                v.tensor_tensor(rows, rows, nrm[:, 1, :].unsqueeze(2).to_broadcast([P, HEADS * NT, P]),
                                ALU.mult).then_inc(out_done, 1)

            def add_residual(n):
                if n == N_IN:
                    v.wait_ge(x_again, 16)
                wait_tile(v, n)
                c, t = (n - N_IN) % 2, (n - N_IN) // 2
                half_row = xr[:, t, c * 512:(c + 1) * 512]
                v.tensor_tensor(half_row, psum[proj_bank(n)][:, :], half_row, ALU.add).then_inc(wo_done, 1)

            for i in range(ALL_STEPS):
                if DONE.get(i, 0) >= N_IN:
                    add_residual(DONE[i])
                if is_real(task(i)):
                    soft(task(i))
                if is_real(task(i - 1)):
                    combine(task(i - 1))
                if task(i - LAG_V) is not None:
                    finish(task(i - LAG_V))
                if i in SPLIT:
                    lo_a(SPLIT[i])

            v.wait_ge(router_in, 32)
            v.tensor_tensor(w_rt, w_rt, g_ffn.unsqueeze(2).to_broadcast([P, KT, E]), ALU.mult).then_inc(router_g, 1)
            v.wait_ge(squares, 6 + NT)
            rsqrt(NT)
            for t in range(NT):
                v.tensor_scalar(xn[:, t, :], xr[:, t, :], nrm[:, 1, t:t + 1], None, ALU.mult).then_inc(normed, 1)

            for t in range(NT):
                v.wait_ge(lg_in, t + 1)
                link(v.tensor_copy(lg[:, t, :], psum[4 + t][:, 0:E]))
                link(v.max(top[:, t, :], lg[:, t, :]))
                link(v.max_index(top_i[:, t, :], top[:, t, :], lg[:, t, :]))
                if t < NT - 1:
                    lo_m(t // 2, t % 2)
            v.tensor_scalar(ntop, top[:, :, 0], -1.0, None, ALU.mult).then_inc(top_ready, 1)
            link(v.tensor_copy(top_f, top_i))
            link(v.tensor_tensor(picked, iota[:, 0:E].unsqueeze(1).unsqueeze(1).to_broadcast([P, NT, TOPK, E]),
                                 top_f[:, :, 0:TOPK].unsqueeze(3).to_broadcast([P, NT, TOPK, E]), ALU.is_equal))
            link(v.tensor_tensor(chosen, picked[:, :, 0, :], picked[:, :, 1, :], ALU.add))
            link(v.tensor_tensor(chosen, chosen, picked[:, :, 2, :], ALU.add))
            v.tensor_tensor(chosen, chosen, picked[:, :, 3, :], ALU.add).then_inc(chosen_ready, 1)
            link(v.memset(cum, 0.0))
            lo_m(1, 1)
            v.wait_ge(rank_in, 1)
            count = psum[0][:, NT * E:(NT + 1) * E]
            link(v.tensor_scalar(n_blk, count, float(P), 1.0, ALU.is_gt, ALU.add))
            for j in (2, 3):
                link(v.scalar_tensor_tensor(out=n_blk, in0=count, scalar=float(P * j), in1=n_blk,
                                            op0=ALU.is_gt, op1=ALU.add))
            link(v.tensor_copy(cum[:, 0, E:2 * E], n_blk))
            cur = 0
            for shift in (1, 2, 4, 8, 16):
                link(v.tensor_tensor(cum[:, 1 - cur, E:2 * E], cum[:, cur, E:2 * E],
                                     cum[:, cur, E - shift:2 * E - shift], ALU.add))
                cur = 1 - cur
            b_end = cum[:, cur, E:2 * E]
            link(v.tensor_tensor(b_start, b_end, n_blk, ALU.subtract))
            for t in range(NT):
                link(v.scalar_tensor_tensor(out=slots[:, t, :], in0=b_start, scalar=float(P),
                                            in1=psum[0][:, t * E:(t + 1) * E], op0=ALU.mult, op1=ALU.add))
            link(v.tensor_tensor(picked_slot, picked, slots.unsqueeze(2).to_broadcast([P, NT, TOPK, E]), ALU.mult))
            link(v.tensor_reduce(slot_f, picked_slot.rearrange("p t k e -> p (t k) e"), AX_X, ALU.add))
            link(v.tensor_copy(slot_i, slot_f))
            link(v.tensor_scalar(loc_i, slot_i, P - 1, None, ALU.bitwise_and))
            link(v.tensor_scalar(blk_i, slot_i, 7, None, ALU.arith_shift_right))
            link(v.tensor_copy(loc_f, loc_i))
            link(v.tensor_copy(blk_f, blk_i))
            v.wait_ge(gates_e, NT)
            link(v.reciprocal(gate_s, gate_s))
            for t in range(NT):
                link(v.tensor_scalar(gate_e[:, t, :], gate_e[:, t, :], gate_s[:, t:t + 1], None, ALU.mult))
            v.wait_ge(ht_out, 2 * NT)
            v.wait_ge(lg_in, NT)
            blocks = iota[:, 0:MAX_BLOCKS]
            link(v.tensor_tensor(e_cmp, blocks.unsqueeze(2).to_broadcast([P, MAX_BLOCKS, E]),
                                 b_end.unsqueeze(1).to_broadcast([P, MAX_BLOCKS, E]), ALU.is_ge))
            link(v.tensor_reduce(exp_f, e_cmp, AX_X, ALU.add))
            link(v.tensor_scalar(exp_f, exp_f, float(E - 1), None, ALU.min))
            link(v.tensor_copy(exp_i, exp_f))
            link(v.tensor_scalar(n_blk[:, 0:1], b_end[:, E - 1:E], 1.0, None, ALU.subtract))
            link(v.tensor_copy(loops_i, n_blk[:, 0:1]))
            pairs = NT * TOPK
            link(v.tensor_tensor(blk_hot[:, :, 2, :], blocks.unsqueeze(1).to_broadcast([P, pairs, MAX_BLOCKS]),
                                 blk_f.unsqueeze(2).to_broadcast([P, pairs, MAX_BLOCKS]), ALU.is_equal))
            v.tensor_tensor(blk_hot[:, :, 1, :], blk_hot[:, :, 2, :],
                            gate_e.rearrange("p t k -> p (t k)").unsqueeze(2).to_broadcast([P, pairs, MAX_BLOCKS]),
                            ALU.mult)
            v.tensor_tensor(blk_hot[:, :, 0, :].rearrange("p (t k) b -> p t k b", k=TOPK),
                            blk_hot[:, :, 2, :].rearrange("p (t k) b -> p t k b", k=TOPK),
                            cst[:, C_TOK:C_TOK + NT].unsqueeze(2).unsqueeze(3).to_broadcast([P, NT, TOPK, MAX_BLOCKS]),
                            ALU.mult)
            for i in range(4):
                v.tensor_tensor(lane_hot[:, 4 * i:4 * i + 4, :], iota.unsqueeze(1).to_broadcast([P, 4, P]),
                                loc_f[:, 4 * i:4 * i + 4].unsqueeze(2).to_broadcast([P, 4, P]),
                                ALU.is_equal).then_inc(hot_ready, 1)
            v.wait_ge(bias_in_s, 64)
            v.wait_ge(half_used, 16)
            v.memset(R[2 * E:P, 4 * D:7 * D].bitcast(F32), 0.0)
            link(v.tensor_copy(bias[0:2 * E, :], bias_in))
            v.tensor_tensor(bias[E:2 * E, :], bias_in[E:2 * E, :], bias[E:2 * E, :].bitcast(F32),
                            ALU.subtract).then_inc(bias_ready, 1)
            v.wait_ge(tab_in, 1)
            link(v.tensor_copy(tok_f, psum[1][:, 0:MAX_BLOCKS]))
            link(v.tensor_copy(gate_t, psum[1][:, MAX_BLOCKS:2 * MAX_BLOCKS]))
            link(v.tensor_scalar(idle_f, tok_f, 0.0, cst[:, C_IDLE:C_IDLE + 1], ALU.is_equal, ALU.mult))
            link(v.scalar_tensor_tensor(out=tok_f, in0=tok_f, scalar=-1.0, in1=idle_f, op0=ALU.add, op1=ALU.add))
            link(v.tensor_copy(sum_row_i, tok_f))
            link(v.tensor_scalar(tok_f, tok_f, float(S - 1), None, ALU.min))
            v.tensor_copy(tok_i, tok_f).then_inc(tab_ready, 1)
            v.wait_ge(tab_ready, 1)

            def turn_x(q, n):
                v.wait_ge(xhi_ready, n)
                bank = psum[6 + q][:, :].rearrange("p (k s) -> p k s", k=4)
                for k in range(4):
                    kk = 4 * q + k
                    ins = v.scalar_tensor_tensor(out=lx[:, kk, :], in0=bank[:, k, :], scalar=g_ffn[:, kk:kk + 1],
                                                 in1=hx[:, kk, :].bitcast(F32), op0=ALU.mult, op1=ALU.subtract)
                ins.then_inc(xlo_ready, 1)

            def turn_act(q, n):
                v.wait_ge(ahi_ready, n)
                v.tensor_tensor(la[:, 4 * q:4 * q + 4, :], psum[6 + q][:, :].rearrange("p (k s) -> p k s", k=4),
                                ha[:, 4 * q:4 * q + 4, :].bitcast(F32), ALU.subtract).then_inc(alo_ready, 1)

            def choose(into, ready, column):
                v.tensor_scalar(into, cst[:, C_ROWMOD:C_ROWMOD + 1].to_broadcast([P, P]), exp_f[:, column], None,
                                ALU.is_equal).then_inc(ready, 1)

            def clamp(c, n):
                v.wait_ge(gu_done, n)
                pairs = psum[c][:, :].rearrange("p (i two) -> p two i", two=2)
                v.tensor_scalar(gate_c[:, c % 2, :], pairs[:, 0, :], LIMIT, None, ALU.min).then_inc(gate_ready, 1)
                v.tensor_scalar(up_c[:, c % 2, :], pairs[:, 1, :], LIMIT, -LIMIT, ALU.min,
                                ALU.max).then_inc(gu_free, 1)
                v.wait_ge(gu_free, n + 4)
                v.scalar_tensor_tensor(out=prod_c[:, c % 2, :], in0=up_c[:, c % 2, :], scalar=1.0,
                                       in1=gate_c[:, c % 2, :], op0=ALU.add, op1=ALU.mult).then_inc(prod_ready, 1)

            def activate(c, n):
                v.wait_ge(sig_ready, n)
                v.wait_ge(prod_ready, n)
                v.tensor_tensor(act[:, c * 256:(c + 1) * 256], prod_c[:, c % 2, :], sig_c[:, c % 2, :],
                                ALU.mult).then_inc(act_ready, 1)

            v.sem_inc(gu_free, 4)
            loops = v.value_load(loops_i[0:1, :], min_val=E - 1, max_val=MAX_LOOPS)
            choose(pick, pick_ready, slice(0, 1))
            turn_x(0, 1)
            turn_x(1, 2)
            lo_m(2, 0)
            lo_m(2, 1)
            clamp(0, 1)
            lo_m(3, 0)
            activate(0, 1)
            lo_m(3, 1)
            clamp(1, 2)
            lo_m(4, 0)
            activate(1, 2)
            lo_m(4, 1)
            clamp(2, 3)
            activate(2, 3)
            turn_x(0, 3)
            turn_x(1, 4)
            v.wait_ge(gu_done, 4)
            choose(pick, pick_ready, slice(1, 2))
            clamp(3, 4)
            activate(3, 4)
            choose(pick_y, pick_y_ready, slice(0, 1))
            lo_m(5, 0)
            turn_act(0, 1)
            lo_m(5, 1)
            clamp(0, 5)
            with v.Fori(1, loops) as b:
                lo_m(0, 0, b)
                turn_act(1, b * 2)
                lo_m(0, 1, b)
                lo_m(1, 0, b)
                activate(0, b * 4 + 1)
                lo_m(1, 1, b)
                clamp(1, b * 4 + 2)
                lo_m(2, 0, b)
                activate(1, b * 4 + 2)
                lo_m(2, 1, b)
                clamp(2, b * 4 + 3)
                lo_m(3, 0, b)
                activate(2, b * 4 + 3)
                turn_x(0, b * 2 + 3)
                lo_m(3, 1, b)
                turn_x(1, b * 2 + 4)
                v.wait_ge(gu_done, b * 4 + 4)
                choose(pick, pick_ready, bass.ds(b + 1, 1))
                lo_m(4, 0, b)
                clamp(3, b * 4 + 4)
                lo_m(4, 1, b)
                activate(3, b * 4 + 4)
                v.wait_ge(ybias_done, b)
                choose(pick_y, pick_y_ready, bass.ds(b, 1))
                lo_m(5, 0, b)
                turn_act(0, b * 2 + 1)
                lo_m(5, 1, b)
                clamp(0, b * 4 + 5)
            b = loops
            lo_m(0, 0, b)
            turn_act(1, b * 2)
            lo_m(0, 1, b)
            lo_m(1, 0, b)
            activate(0, b * 4 + 1)
            lo_m(1, 1, b)
            clamp(1, b * 4 + 2)
            lo_m(2, 0, b)
            activate(1, b * 4 + 2)
            lo_m(2, 1, b)
            clamp(2, b * 4 + 3)
            lo_m(3, 0, b)
            activate(2, b * 4 + 3)
            lo_m(3, 1, b)
            clamp(3, b * 4 + 4)
            v.wait_ge(ybias_done, b)
            choose(pick_y, pick_y_ready, bass.ds(b, 1))
            lo_m(4, 0, b)
            activate(3, b * 4 + 4)
            turn_act(0, b * 2 + 1)
            lo_m(4, 1, b)
            lo_m(5, 0, b)
            turn_act(1, b * 2 + 2)
            lo_m(5, 1, b)

            v.wait_ge(gf_in, 16)
            v.wait_ge(squares, 10 + NT)
            rsqrt(NT)
            for t in range(NT):
                v.scalar_tensor_tensor(out=xr[:, t, :], in0=xr[:, t, :], scalar=nrm[:, 1, t:t + 1], in1=g_final,
                                       op0=ALU.mult, op1=ALU.mult).then_inc(fin_out, 1)

        @block.tensor
        def _(pe):
            def three(bank, a, b, first=False, last=False):
                pe.matmul(bank, a[0], b[0], start=first, stop=False)
                pe.matmul(bank, a[0], b[1], start=False, stop=False)
                return pe.matmul(bank, a[1], b[0], start=False, stop=last)

            def w_part(slot, c0, c1):
                return w_hi[:, slot, c0:c1], w_lo[:, slot, c0:c1]

            def project(n, part=None):
                u, width, turned_out, c0, s0, is_last = TILES[n]
                bank = psum[proj_bank(n)][:, 0:width]
                for k in range(KT) if part is None else range(part * (KT // 2), (part + 1) * (KT // 2)):
                    half = 2 * u + k // 4
                    at0 = k % 4 * UC + c0
                    if k % 4 == 0:
                        pe.wait_ge(lo_ready, half + 1)
                    if turned_out:
                        ins = three(bank, w_part(half % 4, at0, at0 + P),
                                    (act_hi[:, k, s0:s0 + width], act_lo[:, k, s0:s0 + width]), k == 0, k == KT - 1)
                    else:
                        ins = three(bank, (act_hi[:, k, s0:s0 + P], act_lo[:, k, s0:s0 + P]),
                                    w_part(half % 4, at0, at0 + width), k == 0, k == KT - 1)
                    if is_last and k == 3:
                        ins.then_inc(half_used, 1)
                if part != 0:
                    ins.then_inc(half_used if is_last else proj_in, 1)

            def fill(n, part):
                if part != 1:
                    if n < N_IN:
                        pe.wait_ge(proj_out, n)
                    else:
                        pe.wait_ge(mix_lo, NT + (n - N_IN) // 2 + 1)
                        if proj_bank(n) == 0:
                            pe.wait_ge(exp_done, NR)
                        elif n == N_IN:
                            pe.wait_ge(proj_out, n)
                        else:
                            pe.wait_ge(wo_done, n - N_IN)
                project(n, part)

            pe.wait_ge(const_in, 16)
            pe.wait_ge(gains_in, 64)
            pe.transpose(psum[0][:, 0:3 * KT + 1], gain_rows, ident[0:3 * KT + 1, 0:3 * KT + 1]).then_inc(gains_turned, 1)
            pe.wait_ge(gains_ready, 1)
            pe.wait_ge(normed, 2)
            for k in range(KT):
                for t in range(2):
                    ins = pe.transpose(psum[k][:, t * P:(t + 1) * P], mr[:, t, k * P:(k + 1) * P], ident)
                ins.then_inc(turn_in, 1)
            pe.wait_ge(turn_lo, KT)
            for n in range(4):
                project(n)
            pe.wait_ge(normed, 6)
            pe.wait_ge(proj_out, 4)
            for k in range(KT):
                for t in range(NT):
                    ins = pe.transpose(psum[k][:, t * P:(t + 1) * P], xr[:, t, k * P:(k + 1) * P], ident)
                ins.then_inc(turn_in, 1)
            pe.wait_ge(turn_lo, 2 * KT)
            for n in range(4, N_DENSE):
                if n >= 8:
                    pe.wait_ge(proj_out, n - 3)
                project(n)

            pe.wait_ge(proj_out, N_DENSE)
            for i in range(ALL_STEPS):
                t = task(i)
                if is_real(t):
                    kind, h, qb = t
                    r = real[t]
                    if r == HEADS * NT:
                        pe.wait_ge(proj_out, N_IN)
                    n = n_keys(t)
                    if r >= 2:
                        pe.wait_ge(exp_done, r - 1)
                    q0 = qb * P
                    if kind == "diff":
                        for j in range(2):
                            rows = slice(j * DH, (j + 1) * DH)
                            ins = pe.matmul(psum[2 * (r % 2) + j][:, 0:n], qk[rows, h, q0:q0 + P],
                                            qk[rows, 4 + h, 0:n], start=True, stop=True)
                    else:
                        rows = slice(h % 2 * DH, (h % 2 + 1) * DH)
                        q_tile, keys = (8, qk[rows, 10 + h // 2, 0:n]) if kind == "dil" \
                            else (12, mem_k[rows, h // 2, :])
                        ins = pe.matmul(psum[2 * (r % 2)][:, 0:n], qk[rows, q_tile + h // 2, q0:q0 + P], keys,
                                        start=True, stop=True)
                    ins.then_inc(sc_ready, 1)
                if i in FILL:
                    fill(*FILL[i])
                t = task(i - LAG_T)
                if t is not None:
                    ti = turned[t]
                    if ti >= 2:
                        before = by_turn[ti - 2]
                        if before[0] == "mix":
                            pe.wait_ge(mix_lo, NT * before[1] + before[2] + 1)
                        else:
                            pe.wait_ge(pt_out, ti - 1)
                    if t[0] == "mix":
                        last_head = ("diff", HEADS - 1, NT - 1) if t[1] == 0 else ("mem", HEADS - 1, t[2])
                        pe.wait_ge(out_done, real[last_head] + 1)
                        for k in range(4):
                            rows = mix[:, t[2] % 2, k * P:(k + 1) * P] if t[1] else qk[:, k, t[2] * P:(t[2] + 1) * P]
                            ins = pe.transpose(psum[4 + ti % 2][:, k * P:(k + 1) * P], rows, ident)
                    else:
                        r = real[t]
                        pe.wait_ge(prob_ready, r + 1)
                        for kb in range(n_keys(t) // P):
                            ins = pe.transpose(psum[4 + ti % 2][:, kb * P:(kb + 1) * P],
                                               probs[:, r % 2, 0, kb * P:(kb + 1) * P], ident)
                    ins.then_inc(pt_in, 1)
                t = task(i - LAG_V)
                if is_real(t):
                    kind, h, qb = t
                    r = real[t]
                    pe.wait_ge(pt_out, turned[t] + 1)
                    if r >= 1:
                        pe.wait_ge(out_done, r if r <= HEADS * NT else r - 1)
                    nb = n_keys(t) // P
                    for kb in range(nb):
                        values = {"diff": diff_v[:, kb, h * P:(h + 1) * P],
                                  "dil": dil_v[:, kb, h * DH:(h + 1) * DH],
                                  "mem": mem_v[:, kb % 2, h * DH:(h + 1) * DH]}[kind]
                        ins = pe.matmul(psum[out_bank(r)][:, 0:P if kind == "diff" else DH],
                                        pt[:, r % 2, kb * P:(kb + 1) * P], values,
                                        start=kb == 0, stop=kb == nb - 1)
                    ins.then_inc(pv_done, 1)

            pe.wait_ge(exp_done, NR)
            pe.wait_ge(out_done, NR)
            pe.wait_ge(router_in, 32)
            pe.wait_ge(router_g, 1)
            for t in range(NT):
                pe.wait_ge(normed, 6 + t + 1)
                for q in range(2):
                    i = 2 * t + q
                    if i >= 4:
                        pe.wait_ge(ht_out, i - 3)
                    for k in range(4):
                        ins = pe.transpose(psum[i % 4][:, k * P:(k + 1) * P],
                                           xn[:, t, (4 * q + k) * P:(4 * q + k + 1) * P], ident)
                    ins.then_inc(ht_in, 1)
                pe.wait_ge(ht_out, 2 * t + 2)
                for k in range(KT):
                    pe.matmul(psum[4 + t][:, 0:E], hT[:, t % 2, k, :], w_rt[:, k, :], start=k == 0, stop=False)
                pe.matmul(psum[4 + t][:, 0:E], ones[0:1, :], br_row, start=False, stop=True).then_inc(lg_in, 1)
            pe.wait_ge(chosen_ready, 1)
            for t in range(NT):
                bank = psum[0][:, t * E:(t + 1) * E]
                for before in range(t):
                    pe.matmul(bank, ones, chosen[:, before, :], start=before == 0, stop=False)
                pe.matmul(bank, tri, chosen[:, t, :], start=t == 0, stop=True)
            for t in range(NT):
                ins = pe.matmul(psum[0][:, NT * E:(NT + 1) * E], ones, chosen[:, t, :], start=t == 0, stop=t == NT - 1)
            ins.then_inc(rank_in, 1)
            for i in range(NT * TOPK):
                if i % 4 == 0:
                    pe.wait_ge(hot_ready, i // 4 + 1)
                ins = pe.matmul(psum[1][:, 0:2 * MAX_BLOCKS], lane_hot[:, i, :],
                                blk_hot[:, i, 0:2, :].rearrange("p j b -> p (j b)"),
                                start=i == 0, stop=i == NT * TOPK - 1)
            ins.then_inc(tab_in, 1)

            def half_in(m, h, b):
                half = 16 + 2 * m + h
                pe.wait_ge(lo_ready, half + 1 if b is None else b * 12 + (half + 1))
                return half % 4

            def gate_up(m, c, b, n_free, rows=None, n_pick=None, turns=None):
                pe.wait_ge(gu_free, n_free)
                for h in range(2):
                    slot = half_in(m, h, b)
                    if rows is not None:
                        pe.wait_ge(xlo_ready, rows[h])
                    for kk in range(4):
                        k = 4 * h + kk
                        ins = three(psum[c][:, :], (hx[:, k, :], lx[:, k, :]), w_part(slot, kk * UC, (kk + 1) * UC),
                                    first=k == 0)
                    ins.then_inc(half_used, 1)
                    if turns is not None:
                        turn_acts(h, turns[h])
                if n_pick is not None:
                    pe.wait_ge(pick_ready, n_pick)
                pe.matmul(psum[c][:, :], pick, bias[:, c * 512:(c + 1) * 512], start=False,
                          stop=True).then_inc(gu_done, 1)

            def turn_rows(n_h):
                pe.wait_ge(h_in, n_h)
                for k in range(KT):
                    ins = pe.transpose(psum[6 + k // 4][:, k % 4 * P:(k % 4 + 1) * P],
                                       h_row[:, k * P:(k + 1) * P], ident)
                ins.then_inc(xtp_done, 1)

            def turn_acts(q, n):
                pe.wait_ge(act_ready, n)
                for k in range(4):
                    c0 = (4 * q + k) * P
                    ins = pe.transpose(psum[6 + q][:, k * P:(k + 1) * P], act[:, c0:c0 + P], ident)
                ins.then_inc(atp_done, 1)

            def y_bias(b):
                pe.wait_ge(y_free, b + 1)
                pe.wait_ge(pick_y_ready, b + 1)
                for c in range(2):
                    ins = pe.matmul(psum[4 + c][:, :], pick_y, bias[:, 2 * FF + c * 512:2 * FF + (c + 1) * 512],
                                    start=True, stop=False)
                ins.then_inc(ybias_done, 1)

            def down(m, u, b, n_act, turn=None):
                pe.wait_ge(alo_ready, n_act)
                for h in range(2):
                    slot = half_in(m, h, b)
                    for kk in range(2):
                        k = 4 * u + 2 * h + kk
                        for c in range(2):
                            at0 = kk * D + c * 512
                            ins = three(psum[4 + c][:, :], (ha[:, k, :], la[:, k, :]),
                                        w_part(slot, at0, at0 + 512), last=k == KT - 1)
                    ins.then_inc(half_used, 1)
                    if turn is not None and h == 0:
                        turn_acts(1, turn)

            turn_rows(16)
            pe.wait_ge(bias_ready, 1)
            gate_up(0, 0, None, 1, rows=(1, 2), n_pick=1)
            gate_up(1, 1, None, 2)
            turn_rows(32)
            gate_up(2, 2, None, 3)
            gate_up(3, 3, None, 4)
            gate_up(4, 0, None, 5, rows=(3, 4), n_pick=2, turns=(2, 4))
            y_bias(0)
            down(5, 0, None, 1)
            pe.wait_ge(tab_ready, 1)
            loops = pe.value_load(loops_i[0:1, :], min_val=E - 1, max_val=MAX_LOOPS)
            with pe.Fori(1, loops) as b:
                gate_up(0, 1, b, b * 4 + 2)
                pe.wait_ge(alo_ready, b * 2)
                turn_rows(b * 16 + 32)
                gate_up(1, 2, b, b * 4 + 3)
                gate_up(2, 3, b, b * 4 + 4)
                down(3, 1, b, b * 2)
                gate_up(4, 0, b, b * 4 + 5, rows=(b * 2 + 3, b * 2 + 4), n_pick=b + 2, turns=(b * 4 + 2, b * 4 + 4))
                y_bias(b)
                down(5, 0, b, b * 2 + 1)
            b = loops
            gate_up(0, 1, b, b * 4 + 2)
            gate_up(1, 2, b, b * 4 + 3)
            gate_up(2, 3, b, b * 4 + 4)
            down(3, 1, b, b * 2)
            turn_acts(0, b * 4 + 2)
            y_bias(b)
            down(4, 0, b, b * 2 + 1, turn=b * 4 + 4)
            down(5, 1, b, b * 2 + 2)


_INS = ["x", "mem", "attn_norm_g", "mem_norm_g", "w_in", "diff_lambda_qk", "diff_subln_g", "w_mem_kv", "w_out",
        "ffn_norm_g", "w_router", "b_router", "w_gate_up", "b_gate_up", "w_down", "b_down", "final_norm_g"]


def kernel(**inputs):
    import concourse.bacc as bacc
    from concourse.bass_utils import run_bass_kernel_spmd

    nc = bacc.Bacc("TRN2", target_bir_lowering=False, num_devices=1)
    given = {name: np.ascontiguousarray(inputs[name]) for name in _INS}
    given["constants"] = constants()
    given["position_tables"] = position_tables()
    arrays, args = {}, []
    for name, a in given.items():
        arrays[f"in_{name}_dram"] = a
        args.append(nc.dram_tensor(f"in_{name}_dram", a.shape, mybir.dt.from_np(a.dtype), kind="ExternalInput").ap())
    args.append(nc.dram_tensor("out_0_dram", (1, S, D), F32, kind="ExternalOutput").ap())
    hymba_layer(nc, *args)
    r = run_bass_kernel_spmd(nc, [arrays], core_ids=[0])
    return r.results[0]["out_0_dram"]
```
